# Optimizing a Trainium2 kernel written in Bass

```python
import jax, jax.numpy as jnp
from jax import lax
import numpy as np

D_MODEL = 1024
BATCH = 1
SEQ = 128
DEPTH = 2
DEC_BATCH = 1
DEC_SEQ = 256
PAST_LEN = 128

GRID_W = 64
N_MIXERS = 2
N_CONV_LAYERS = (DEPTH + 1) // 2
N_MLA_LAYERS = DEPTH // 2
N_MOD = 6
CONV_WIDTH = 31
CONV_PAD = CONV_WIDTH // 2
N_HEADS = 16
QK_NOPE_DIM = 128
ROPE_DIM = 64
QK_HEAD_DIM = QK_NOPE_DIM + ROPE_DIM
V_HEAD_DIM = 128
Q_LORA_RANK = 512
KV_LORA_RANK = 256
AXIS_ROPE_DIM = ROPE_DIM // 2
ROPE_BASE = 10000.0
Q_BLOCK = 128
D_FF = 2816
N_EXPERTS = 8
TOP_K = 2
D_FF_EXPERT = 1536
EPS = 1e-6
F32 = jnp.float32

kernel_name = 'hybrid_conv_mla_diffusion_step'

def rms_norm(x, g):
    x32 = x.astype(F32)
    y = x32 * lax.rsqrt(jnp.mean(x32 * x32, axis=-1, keepdims=True) + EPS)
    return (y * g.astype(F32)).astype(x.dtype)

def layer_norm(x, g, b):
    x32 = x.astype(F32)
    mu = jnp.mean(x32, axis=-1, keepdims=True)
    xc = x32 - mu
    y = xc * lax.rsqrt(jnp.mean(xc * xc, axis=-1, keepdims=True) + EPS)
    return (y * g.astype(F32) + b.astype(F32)).astype(x.dtype)

def adaln(cond, w, b):
    m = jax.nn.silu(cond) @ w + b
    return jnp.split(m[:, None, :], N_MOD, axis=-1)

def modulate(h, shift, scale):
    return h * (1 + scale) + shift

def axial_rope_tables(n_tokens):
    rows = n_tokens // GRID_W
    row = jnp.repeat(jnp.arange(rows), GRID_W).astype(F32)
    col = jnp.tile(jnp.arange(GRID_W), rows).astype(F32)
    inv = ROPE_BASE ** (-jnp.arange(0, AXIS_ROPE_DIM, 2, dtype=F32) / AXIS_ROPE_DIM)
    ang = jnp.stack([row[:, None] * inv, col[:, None] * inv], axis=1)
    return jnp.cos(ang), jnp.sin(ang)

def apply_axial_rope(x, cos, sin):
    xr = x.reshape(x.shape[:-1] + (2, 2, AXIS_ROPE_DIM // 2))
    x1, x2 = xr[..., 0, :], xr[..., 1, :]
    c = cos[None, :, None].astype(x.dtype)
    s = sin[None, :, None].astype(x.dtype)
    out = jnp.stack([x1 * c - x2 * s, x1 * s + x2 * c], axis=-2)
    return out.reshape(x.shape)

def rope_tail(t, cos, sin):
    return jnp.concatenate([t[..., :QK_NOPE_DIM], apply_axial_rope(t[..., QK_NOPE_DIM:], cos, sin)], axis=-1)

def conv_module(h, pw1, dw, dw_b, ln_g, ln_b, pw2):
    a, g = jnp.split(h @ pw1, 2, axis=-1)
    u = a * jax.nn.sigmoid(g)
    u = lax.conv_general_dilated(u, dw[:, None, :], window_strides=(1,), padding=[(CONV_PAD, CONV_PAD)],
                                 dimension_numbers=('NWC', 'WIO', 'NWC'), feature_group_count=D_MODEL) + dw_b
    u = jax.nn.silu(layer_norm(u, ln_g, ln_b))
    return u @ pw2

def mla_query(h, wdq, q_norm_g, wuq, q_qk_g):
    b, s, _ = h.shape
    cq = rms_norm(h @ wdq, q_norm_g)
    q = (cq @ wuq).reshape(b, s, N_HEADS, QK_HEAD_DIM)
    return rms_norm(q, q_qk_g)

def mla_compress(h, wdkv, kv_norm_g):
    kv_a = h @ wdkv
    ckv = rms_norm(kv_a[..., :KV_LORA_RANK], kv_norm_g)
    krope = kv_a[..., KV_LORA_RANK:]
    return ckv, krope

def mla_expand(ckv, krope, wukv, k_qk_g):
    b, s, _ = ckv.shape
    kv = (ckv @ wukv).reshape(b, s, N_HEADS, QK_NOPE_DIM + V_HEAD_DIM)
    k_nope, v = kv[..., :QK_NOPE_DIM], kv[..., QK_NOPE_DIM:]
    k = jnp.concatenate([k_nope, jnp.broadcast_to(krope[:, :, None, :], (b, s, N_HEADS, ROPE_DIM))], axis=-1)
    return rms_norm(k, k_qk_g), v

def attention(q, k, v):
    b, sq, h, dk = q.shape
    nb = sq // Q_BLOCK
    qb = q.reshape(b, nb, Q_BLOCK, h, dk).transpose(1, 0, 2, 3, 4)
    scale = QK_HEAD_DIM ** -0.5

    def block(qi):
        s = jnp.einsum('bqhd,bkhd->bhqk', qi, k).astype(F32) * scale
        p = jax.nn.softmax(s, axis=-1).astype(v.dtype)
        return jnp.einsum('bhqk,bkhd->bqhd', p, v)

    o = lax.map(block, qb)
    return o.transpose(1, 0, 2, 3, 4).reshape(b, sq, h * V_HEAD_DIM)

def swiglu(t, w1, w3, w2):
    return (jax.nn.silu(t @ w1) * (t @ w3)) @ w2

def moe_swiglu(h, w_router, w1, w3, w2):
    b, s, d = h.shape
    t = h.reshape(b * s, d)
    logits = (t @ w_router).astype(F32)
    top_v, top_i = lax.top_k(logits, TOP_K)
    top_w = jax.nn.softmax(top_v, axis=-1)
    gates = jnp.sum(jax.nn.one_hot(top_i, N_EXPERTS, dtype=F32) * top_w[..., None], axis=-2).astype(t.dtype)
    out = jnp.zeros_like(t)
    for e in range(N_EXPERTS):
        out = out + gates[:, e:e + 1] * swiglu(t, w1[e], w3[e], w2[e])
    return out.reshape(b, s, d)

def setup_inputs(seed: int = 0) -> dict:
    key = jax.random.key(seed)
    ks = iter(jax.random.split(key, 48))
    D = D_MODEL
    NC = N_CONV_LAYERS
    NM = N_MLA_LAYERS

    def w(shape, fan_in, mult=1.0):
        return jax.random.normal(next(ks), shape, F32) * (mult * fan_in ** -0.5)

    def gain(shape):
        return 1.0 + 0.1 * jax.random.normal(next(ks), shape, F32)

    def bias(shape):
        return 0.02 * jax.random.normal(next(ks), shape, F32)

    def nrm(shape):
        return jax.random.normal(next(ks), shape, F32)

    return {
        'x_prompt': nrm((BATCH, SEQ, D)),
        'x_sample': nrm((DEC_BATCH, DEC_SEQ, D)),
        'c': nrm((DEC_BATCH, D)),
        'cache_ckv': nrm((DEC_BATCH, NM, PAST_LEN, KV_LORA_RANK)),
        'cache_krope': nrm((DEC_BATCH, NM, PAST_LEN, ROPE_DIM)),
        'c_ctx': nrm((D,)),
        'ada_w': w((DEPTH, D, N_MOD * D), D, 0.5),
        'ada_b': bias((DEPTH, N_MOD * D)),
        'norm1_g': gain((DEPTH, D)),
        'norm2_g': gain((DEPTH, D)),
        'conv_pw1': w((NC, D, 2 * D), D),
        'conv_dw': w((NC, CONV_WIDTH, D), CONV_WIDTH),
        'conv_dw_b': bias((NC, D)),
        'conv_ln_g': gain((NC, D)),
        'conv_ln_b': bias((NC, D)),
        'conv_pw2': w((NC, D, D), D),
        'ffn_w1': w((NC, D, D_FF), D),
        'ffn_w3': w((NC, D, D_FF), D),
        'ffn_w2': w((NC, D_FF, D), D_FF),
        'mla_wdq': w((NM, D, Q_LORA_RANK), D),
        'mla_q_norm_g': gain((NM, Q_LORA_RANK)),
        'mla_wuq': w((NM, Q_LORA_RANK, N_HEADS * QK_HEAD_DIM), Q_LORA_RANK),
        'mla_wdkv': w((NM, D, KV_LORA_RANK + ROPE_DIM), D),
        'mla_kv_norm_g': gain((NM, KV_LORA_RANK)),
        'mla_wukv': w((NM, KV_LORA_RANK, N_HEADS * (QK_NOPE_DIM + V_HEAD_DIM)), KV_LORA_RANK),
        'mla_q_qk_g': gain((NM, QK_HEAD_DIM)),
        'mla_k_qk_g': gain((NM, QK_HEAD_DIM)),
        'mla_wo': w((NM, N_HEADS * V_HEAD_DIM, D), N_HEADS * V_HEAD_DIM),
        'moe_router': w((NM, D, N_EXPERTS), D),
        'moe_w1': w((NM, N_EXPERTS, D, D_FF_EXPERT), D),
        'moe_w3': w((NM, N_EXPERTS, D, D_FF_EXPERT), D),
        'moe_w2': w((NM, N_EXPERTS, D_FF_EXPERT, D), D_FF_EXPERT),
    }

def reference(x_prompt, x_sample, c, cache_ckv, cache_krope, c_ctx, ada_w, ada_b, norm1_g, norm2_g,
              conv_pw1, conv_dw, conv_dw_b, conv_ln_g, conv_ln_b, conv_pw2, ffn_w1, ffn_w3, ffn_w2,
              mla_wdq, mla_q_norm_g, mla_wuq, mla_wdkv, mla_kv_norm_g, mla_wukv, mla_q_qk_g, mla_k_qk_g,
              mla_wo, moe_router, moe_w1, moe_w3, moe_w2):
    cos, sin = axial_rope_tables(x_sample.shape[1])
    xp, xs = x_prompt, x_sample
    new_ckv, new_krope = [], []
    for i in range(DEPTH):
        j = i // N_MIXERS
        mp = adaln(c_ctx[None, :], ada_w[i], ada_b[i])
        ms = adaln(c, ada_w[i], ada_b[i])
        hp = modulate(rms_norm(xp, norm1_g[i]), mp[0], mp[1])
        hs = modulate(rms_norm(xs, norm1_g[i]), ms[0], ms[1])
        if i % N_MIXERS == 0:
            op = conv_module(hp, conv_pw1[j], conv_dw[j], conv_dw_b[j], conv_ln_g[j], conv_ln_b[j], conv_pw2[j])
            os_ = conv_module(hs, conv_pw1[j], conv_dw[j], conv_dw_b[j], conv_ln_g[j], conv_ln_b[j], conv_pw2[j])
        else:
            ckv_p, krope_p = mla_compress(hp, mla_wdkv[j], mla_kv_norm_g[j])
            new_ckv.append(ckv_p)
            new_krope.append(krope_p)
            kp, vp = mla_expand(ckv_p, krope_p, mla_wukv[j], mla_k_qk_g[j])
            qp = mla_query(hp, mla_wdq[j], mla_q_norm_g[j], mla_wuq[j], mla_q_qk_g[j])
            op = attention(qp, kp, vp) @ mla_wo[j]
            kc, vc = mla_expand(cache_ckv[:, j], cache_krope[:, j], mla_wukv[j], mla_k_qk_g[j])
            ckv_s, krope_s = mla_compress(hs, mla_wdkv[j], mla_kv_norm_g[j])
            ks, vs = mla_expand(ckv_s, krope_s, mla_wukv[j], mla_k_qk_g[j])
            ks = rope_tail(ks, cos, sin)
            qs = rope_tail(mla_query(hs, mla_wdq[j], mla_q_norm_g[j], mla_wuq[j], mla_q_qk_g[j]), cos, sin)
            os_ = attention(qs, jnp.concatenate([ks, kc], axis=1), jnp.concatenate([vs, vc], axis=1)) @ mla_wo[j]
        xp = xp + mp[2] * op
        xs = xs + ms[2] * os_
        hp = modulate(rms_norm(xp, norm2_g[i]), mp[3], mp[4])
        hs = modulate(rms_norm(xs, norm2_g[i]), ms[3], ms[4])
        if i % 2 == 0:
            fp = swiglu(hp, ffn_w1[j], ffn_w3[j], ffn_w2[j])
            fs = swiglu(hs, ffn_w1[j], ffn_w3[j], ffn_w2[j])
        else:
            fp = moe_swiglu(hp, moe_router[j], moe_w1[j], moe_w3[j], moe_w2[j])
            fs = moe_swiglu(hs, moe_router[j], moe_w1[j], moe_w3[j], moe_w2[j])
        xp = xp + mp[5] * fp
        xs = xs + ms[5] * fs
    return (xp, xs, jnp.stack(new_ckv, axis=1), jnp.stack(new_krope, axis=1))


_drawn_inputs = setup_inputs


def setup_inputs(seed=0):
    import zlib

    import numpy as np

    out = dict(_drawn_inputs(seed))
    spreads = {}
    factors = {'cache_ckv': 3.126,
     'cache_krope': 4.005,
     'conv_dw_b': 3.602,
     'conv_ln_b': 5.497,
     'mla_q_norm_g': 5.183,
     'mla_q_qk_g': 4.236,
     'mla_k_qk_g': 7.446}
    for name, (base, spread) in spreads.items():
        noise = np.random.default_rng([zlib.crc32(name.encode()), seed]).standard_normal(out[name].shape)
        drawn = base * np.exp(spread * noise) if base else spread * noise
        out[name] = __import__('jax').numpy.asarray(drawn.astype(out[name].dtype))
    for name, factor in factors.items():
        out[name] = (out[name] * factor).astype(out[name].dtype)
    return out
```

```python
import numpy as np
from contextlib import ExitStack

import concourse.bass as bass
from concourse import mybir

F32 = mybir.dt.float32
F32R = mybir.dt.float32r
I32 = mybir.dt.int32
ALU = mybir.AluOpType
ACT = mybir.ActivationFunctionType
AX = mybir.AxisListType.X
ds = bass.ds

P = 128
EPS = 1e-6
GRID_W = 64
ROPE_BASE = 10000.0
TOP_K = 2
CH = 2048
RAW = 6
HL = 3
BIG = 1000.0
GONE = -3.0e38
MAGIC = 0x5F3759DF


def at(v, loop=None, times=1):
    return v if loop is None else loop[0] * (loop[1] * times) + v


class Steps:

    def __init__(self, eng, sem):
        self.eng, self.sem, self.n, self.loop = eng, sem, 0, None

    def __call__(self, ins):
        ins.then_inc(self.sem, 1)
        self.n += 1
        self.eng.wait_ge(self.sem, at(self.n, self.loop))

    def begin(self, reg, per):
        self.loop, self.first, self.per = (reg, per), self.n, per

    def end(self, turns):
        assert self.n - self.first == self.per, (self.n - self.first, self.per)
        self.loop, self.n = None, self.first + self.per * turns


def hybrid_conv_mla_diffusion_step(nc, d, out):
    DEPTH, D, _ = d["ada_w"].shape
    DK = D // P
    NP_TOK = d["x_prompt"].shape[1]
    NS_TOK = d["x_sample"].shape[1]
    T = NP_TOK + NS_TOK
    TC = T // P
    PAST = d["cache_ckv"].shape[2]
    CW = d["conv_dw"].shape[1]
    PAD = CW // 2
    CU = PAD + NP_TOK + PAD + NS_TOK + PAD
    CV = CU - 2 * PAD
    SV = NP_TOK + PAD
    FF = d["ffn_w1"].shape[2]
    NF = FF // P
    QLR = d["mla_wdq"].shape[2]
    KVR = d["mla_kv_norm_g"].shape[1]
    QKD = d["mla_q_qk_g"].shape[1]
    RD = QKD - P
    NH = d["mla_wuq"].shape[2] // QKD
    NE = d["moe_router"].shape[2]
    FE = d["moe_w1"].shape[3]
    NG = FE // 512
    KC = (T + PAST) // P
    NX = (TOP_K * T - 1) // P
    NT = NE + NX + 1
    assert (DK, TC, KC, NP_TOK, QKD, KVR, QLR, NG) == (8, 3, 4, P, 192, 256, 512, 3)

    ADA_CH = 6 * D // 512 * 2
    PW1 = ADA_CH
    ADA1 = PW1 + 2 * D // 256
    PW2 = ADA1 + ADA_CH
    FFN = PW2 + DK // 2
    MLA = FFN + 3 * (NF // 2)
    GRP = MLA + 4
    NGRP = NH // 4
    MOE = GRP + 6 * NGRP
    TILE_CH = 6 * NG
    MOEX = MOE + TILE_CH * NE

    ctx = ExitStack()
    with ctx:
        def sb(name, shape, dt=F32):
            return ctx.enter_context(nc.sbuf_tensor(name, shape, dt))

        def share(name, *groups):
            made, most = [], 0
            for group in groups:
                with ExitStack() as s:
                    made.append([s.enter_context(nc.sbuf_tensor(n, shape, dt)) for n, shape, dt in group])
                most = max(most, sum(-(-int(np.prod(shape[1:])) * 4 // 64) * 16 for _, shape, _ in group))
            sb(name, [P, most])
            return made

        raw = sb("raw", [P, RAW, CH])
        wh = sb("wh", [P, HL, CH], F32R)
        wl = sb("wl", [P, HL, CH], F32R)
        x = sb("x", [P, TC, D])
        ident = sb("ident", [P, P])
        ones = sb("ones", [P, P])
        vT = sb("vT", [P, 80])
        modv = sb("modv", [P, DEPTH, 2, 4, DK])
        modA = sb("modA", [P, DEPTH, 2, 2, DK])
        st = sb("st", [P, 64])
        nr = sb("nr", [P, 3, 16])
        nri = sb("nri", [P, 2, 16], I32)
        comb = sb("comb", [5, 2])
        epsc = sb("epsc", [P, 1])

        (gate,), (pr,) = share(
            "shared8",
            [("gate", [P, 2, D], F32)],
            [("pr", [P, 2, 7 * P], F32)])
        (mrow,), (hTh, hTl), (cqTh, cqTl, ckTh, ckTl, kr_rot, tq), (xgh, xgl, hm, hgh, hgl) = share(
            "shared24",
            [("mrow", [P, 6 * D], F32)],
            [("hTh", [P, DK, T], F32R), ("hTl", [P, DK, T], F32R)],
            [("cqTh", [P, 4, T], F32R), ("cqTl", [P, 4, T], F32R), ("ckTh", [P, 2, KC * P], F32R),
             ("ckTl", [P, 2, KC * P], F32R), ("kr_rot", [P, KC, RD], F32), ("tq", [P, 2, 2 * TC, RD], F32)],
            [("xgh", [P, DK, P], F32R), ("xgl", [P, DK, P], F32R), ("hm", [P, 2, 512], F32),
             ("hgh", [P, FE // P, P], F32R), ("hgl", [P, FE // P, P], F32R)])
        (xn,), (v,), (kv_sb, krh, KR) = share(
            "shared12a",
            [("xn", [P, TC, D], F32)],
            [("v", [P, DK, CV], F32)],
            [("kv_sb", [P, KC, 512], F32), ("krh", [P, KC, 2, RD], F32), ("KR", [P, KC * P], F32)])
        (hf,), (yacc,), (cqf, ckv) = share(
            "shared12b",
            [("hf", [P, DK, T], F32)],
            [("yacc", [P, TC, D], F32)],
            [("cqf", [P, 4, T], F32), ("ckv", [P, KC, KVR + RD], F32)])
        ((vec, cst, mT, grow, dwT, u, sig), (_, _, _, _, _, _, sq, sd, rs), (fs, ff, fh, fl),
         (q_sb, qr, KT, QB, pT, oTh, oTl, tk, gb),
         (yh, yl, sel, selT, ms, R, G, rt, jt, tab, before, iota, router)) = share(
            "own",
            [("vec", [P, 3, P], F32), ("cst", [P, DK, P], F32R), ("mT", [P, 32, 5], F32), ("grow", [2, 4, 512], F32),
             ("dwT", [P, CW * DK], F32), ("u", [P, DK, CU], F32), ("sig", [P, 2, 2, T], F32)],
            [("vec_", [P, 3, P], F32), ("cst_", [P, DK, P], F32R), ("mT_", [P, 32, 5], F32),
             ("grow_", [2, 4, 512], F32), ("dwT_", [P, CW * DK], F32), ("u_", [P, DK, CU], F32),
             ("sq", [P, 2, CV], F32), ("sd", [P, CV], F32), ("rs", [P, CV], F32)],
            [("fs", [P, 2, T], F32), ("ff", [P, 2, T], F32), ("fh", [P, 2, T], F32R), ("fl", [P, 2, T], F32R)],
            [("q_sb", [P, 2 * TC, QKD], F32), ("qr", [P, 2, 2 * TC, RD], F32), ("KT", [P, 2, KC * P], F32),
             ("QB", [P, 3, T], F32), ("pT", [P, 7 * P], F32), ("oTh", [P, 4, T], F32R), ("oTl", [P, 4, T], F32R),
             ("tk", [P, 2, KC, RD], F32), ("gb", [P, 2 * RD + KVR], F32)],
            [("yh", [P, D], F32R), ("yl", [P, D], F32R), ("sel", [P, TC, P], F32), ("selT", [P, T], F32R),
             ("ms", [P, 512], F32), ("R", [P, TC, NT], F32), ("G", [P, TC, NT + 1], F32),
             ("rt", [P, 12, TC, NE], F32), ("jt", [P, 12, NE], F32), ("tab", [1, 16], I32),
             ("before", [P, P], F32), ("iota", [P, P], F32), ("router", [P, DK, NE], F32)])
        ps = ctx.enter_context(nc.psum_tensor("ps", [P, 8, 512], F32))
        gates_dram = nc.dram_tensor("gates_dram", [DEPTH, 2, 2, D], F32, kind="Internal").ap()

        N1G, N2G, DWB, LNG, LNB, QNG, QKG, KKG, CND = 0, 16, 32, 40, 48, 56, 62, 63, 64
        VROWS = [("norm1_g", None), ("norm2_g", None), ("conv_dw_b", None), ("conv_ln_g", None), ("conv_ln_b", None),
                 ("mla_q_norm_g", None), ("mla_kv_norm_g", None)]

        named = {}

        def sem(name):
            if name not in named:
                named[name] = ctx.enter_context(nc.semaphore(name))
            return named[name]

        raw_in = [sem(f"raw_in{i}") for i in range(RAW)]
        hi_made, lo_made = sem("hi_made"), sem("lo_made")
        chunk_used = sem("chunk_used")

        def load(sp, s, src, view, loop=None):
            if s >= RAW or loop:
                sp.wait_ge(hi_made, at(s - RAW + 1, loop))
                sp.wait_ge(lo_made, at(s - RAW + 1, loop))
            sp.dma_start(view(raw[:, s % RAW, :]), src).then_inc(raw_in[s % RAW], 16)

        def make_hi(act, s, loop=None):
            turns = None if loop is None else (loop[0], loop[1] // RAW * 16)
            act.wait_ge(raw_in[s % RAW], at(16 * (s // RAW + 1), turns))
            if s >= HL or loop:
                act.wait_ge(chunk_used, at(s - HL + 1, loop))
            act.activation(wh[:, s % HL, :], raw[:, s % RAW, :], ACT.Copy).then_inc(hi_made, 1)

        def make_lo(eng, s, loop=None):
            eng.wait_ge(hi_made, at(s + 1, loop))
            if s >= HL or loop:
                eng.wait_ge(chunk_used, at(s - HL + 1, loop))
            eng.tensor_tensor(wl[:, s % HL, :], raw[:, s % RAW, :], wh[:, s % HL, :],
                              ALU.subtract).then_inc(lo_made, 1)

        def parts(s, n, k):
            return [t[:, s % HL, 0:k * n].rearrange("p (k n) -> p k n", k=k) for t in (wh, wl)]

        def rows(w, k0, k, c0, n):
            return w.rearrange("(k p) n -> p k n", p=P)[:, k0:k0 + k, c0:c0 + n]

        def as_rows(n, k):
            return lambda slot: slot[:, 0:k * n].rearrange("p (k n) -> p k n", k=k)

        def mm3(out_, sh, sl, mh, ml, start, stop):
            nc.tensor.matmul(out_, sh, mh, start=start, stop=False)
            nc.tensor.matmul(out_, sh, ml, start=False, stop=False)
            return nc.tensor.matmul(out_, sl, mh, start=False, stop=stop)

        def rsqrt(step, dst, src, n, shape=None):
            a, b, y = nr[:, 0, 0:n], nr[:, 1, 0:n], nr[:, 2, 0:n]
            dve = nc.vector
            step(dve.tensor_scalar(a, src, EPS, None, ALU.add))
            step(dve.tensor_scalar(nri[:, 0, 0:n], a.bitcast(I32), 1, None, ALU.logical_shift_right))
            step(dve.tensor_scalar(y.bitcast(I32), nri[:, 0, 0:n], -1, MAGIC, ALU.mult, ALU.add))
            for i in range(4):
                step(dve.tensor_tensor(b, y, y, ALU.mult))
                step(dve.scalar_tensor_tensor(out=b, in0=b, scalar=-0.5, in1=a, op0=ALU.mult, op1=ALU.mult))
                step(dve.scalar_tensor_tensor(out=y if i < 3 else dst, in0=b, scalar=1.5, in1=y,
                                              op0=ALU.add, op1=ALU.mult))

        RSQRT_STEPS = 15

        def norm_act(act, q, layer, n, before_, count):
            act.wait_ge(sem(before_), count)
            for c in range(TC):
                act.activation(xn[:, c, :], x[:, c, :], ACT.Square, scale=D ** -0.5,
                               accum_out=st[:, c:c + 1]).then_inc(sem(q + "_squares"), 1)
            act.wait_ge(sem(f"mod_ready{layer}"), 1)
            for j in range(DK):
                act.wait_ge(sem(q + "_turned"), j + 1)
                for cond, a, b in ((1, 0, P), (0, P, T)):
                    act.activation(hf[:, j, a:b], ps[:, 6 + j % 2, a:b], ACT.Identity,
                                   scale=modA[:, layer, n, cond, j:j + 1],
                                   bias=modv[:, layer, cond, 2 * n, j:j + 1]).then_inc(sem(q + "_modulated"), 1)

        def norm_dve(dve, step, q):
            dve.wait_ge(sem(q + "_squares"), TC)
            rsqrt(step, st[:, 4:4 + TC], st[:, 0:TC], TC)
            for c in range(TC):
                dve.tensor_scalar(xn[:, c, :], x[:, c, :], st[:, 4 + c:5 + c], None,
                                  ALU.mult).then_inc(sem(q + "_normed"), 1)

        def norm_pe(pe, q):
            pe.wait_ge(sem(q + "_normed"), TC)
            for j in range(DK):
                if j >= 2:
                    pe.wait_ge(sem(q + "_modulated"), 2 * (j - 1))
                for c in range(TC):
                    last = pe.transpose(ps[:, 6 + j % 2, c * P:(c + 1) * P], xn[:, c, j * P:(j + 1) * P], ident[:, :])
                last.then_inc(sem(q + "_turned"), 1)

        def split_dve(dve, q, made, per):
            for j in range(DK):
                dve.wait_ge(sem(made), per * (j + 1))
                dve.tensor_copy(hTh[:, j, :], hf[:, j, :]).then_inc(sem(q + "_h_hi"), 1)
                dve.wait_ge(sem(q + "_h_hi"), j + 1)
                dve.tensor_tensor(hTl[:, j, :], hf[:, j, :], hTh[:, j, :], ALU.subtract).then_inc(sem(q + "_h_lo"), 1)

        def residual(dve, step, q, y):
            for c in range(TC):
                step(dve.tensor_tensor(xn[:, c, :], y(c), gate[:, 1 if c == 0 else 0, :], ALU.mult))
                dve.tensor_tensor(x[:, c, :], x[:, c, :], xn[:, c, :], ALU.add).then_inc(sem(q + "_x"), 1)
            dve.wait_ge(sem(q + "_x"), TC)

        block = ctx.enter_context(nc.Block())

        @block.sync
        def _(sp):
            for layer, base in ((0, 0), (1, ADA1)):
                if layer == 1:
                    for t in range(4):
                        for i in range(2):
                            load(sp, PW1 + 2 * t + i, rows(d["conv_pw1"][0], 0, DK, i * D + t * 256, 256), as_rows(256, DK))
                w = d["ada_w"][layer].rearrange("(k p) n -> p k n", p=P)
                first = 0
                if layer == 0:
                    for k in range(6):
                        load(sp, k, w[:, 4 * (k % 2):4 * (k % 2) + 4, 512 * (k // 2):512 * (k // 2) + 512], as_rows(512, 4))
                    first = 1
                with sp.Fori(first, 4) as it:
                    for k in range(6):
                        load(sp, base + k, w[:, 4 * (k % 2):4 * (k % 2) + 4, ds(it * 1536 + 512 * (k // 2), 512)],
                             as_rows(512, 4), (it, 6))
            for q in range(DK // 2):
                load(sp, PW2 + q, rows(d["conv_pw2"][0], 2 * q, 2, 0, D), as_rows(D, 2))
            w1, w3 = (d[n][0].rearrange("(k p) n -> p k n", p=P) for n in ("ffn_w1", "ffn_w3"))
            w2 = d["ffn_w2"][0].rearrange("(k p) n -> p k n", p=P)
            with sp.Fori(0, 5) as it:
                for i in range(2):
                    s = FFN + 3 * i
                    load(sp, s, w1[:, :, ds(it * 512 + 256 * i, 256)], as_rows(256, DK), (it, 6))
                    load(sp, s + 1, w3[:, :, ds(it * 512 + 256 * i, 256)], as_rows(256, DK), (it, 6))
                    load(sp, s + 2, w2[:, ds(it * 4 + 2 * i, 2), :], as_rows(D, 2), (it, 6))
            s = FFN + 30
            load(sp, s, w1[:, :, FF - 256:FF], as_rows(256, DK))
            load(sp, s + 1, w3[:, :, FF - 256:FF], as_rows(256, DK))
            load(sp, s + 2, w2[:, NF - 2:NF, :], as_rows(D, 2))
            for i in range(2):
                load(sp, MLA + i, rows(d["mla_wdq"][0], 4 * i, 4, 0, QLR), as_rows(QLR, 4))
            for i in range(2):
                load(sp, MLA + 2 + i, rows(d["mla_wdkv"][0], 4 * i, 4, 0, KVR + RD), as_rows(KVR + RD, 4))
            wuq, wukv, wo = (d[n][0].rearrange("(k p) n -> p k n", p=P) for n in ("mla_wuq", "mla_wukv", "mla_wo"))
            with sp.Fori(0, NGRP) as g:
                for i in range(2):
                    load(sp, GRP + 2 * i, wukv[:, :, ds(g * 1024 + 512 * i, 512)], as_rows(512, 2), (g, 6))
                    load(sp, GRP + 2 * i + 1, wuq[:, :, ds(g * 768 + 384 * i, 384)], as_rows(384, 4), (g, 6))
                for i in range(2):
                    load(sp, GRP + 4 + i, wo[:, ds(g * 4, 4), i * 512:i * 512 + 512], as_rows(512, 4), (g, 6))

            ew1, ew3 = (d[n][0].rearrange("e (k p) n -> p e k n", p=P) for n in ("moe_w1", "moe_w3"))
            ew2 = d["moe_w2"][0].rearrange("e (k p) n -> p e k n", p=P)

            def load_tile(t, e):
                for g in range(NG):
                    for i in range(4):
                        w = (ew1, ew3)[i // 2]
                        load(sp, MOE + 4 * g + i, w[:, e, 4 * (i % 2):4 * (i % 2) + 4, 512 * g:512 * g + 512],
                             as_rows(512, 4), (t, TILE_CH))
                for i in range(6):
                    load(sp, MOE + 4 * NG + i, ew2[:, e, 2 * i:2 * i + 2, :], as_rows(D, 2), (t, TILE_CH))

            with sp.Fori(0, NE) as e:
                load_tile(e, e)
            sp.wait_ge(sem("tab_ready"), 1)
            more = sp.value_load(tab[0:1, 0:1], min_val=0, max_val=NX)
            with sp.Fori(0, NX) as j:
                with sp.If(j < more):
                    load_tile(j + NE, sp.value_load(tab[0:1, ds(j + 1, 1)], min_val=0, max_val=NE - 1))
            for c in range(TC):
                sp.wait_ge(sem("moe_x"), c + 1)
                dst = out["y_prompt"][0] if c == 0 else out["y_sample"][0, (c - 1) * P:c * P, :]
                sp.dma_start(dst, x[:, c, :]).then_inc(sem("y_out"), 16)
            sp.wait_ge(sem("y_out"), 16 * TC)
            sp.wait_ge(sem("kv_out"), 32)

        @block.gpsimd
        def _(pool):
            pool.memset(ident[:, :], 0.0).then_inc(sem("pool_steps"), 1)
            pool.memset(ones[:, :], 1.0).then_inc(sem("ones_made"), 1)
            pool.memset(epsc[:, :], EPS).then_inc(sem("ones_made"), 1)
            pool.memset(cst[:, :, :].bitcast(F32), 0.0).then_inc(sem("cst_zero"), 1)
            pool.wait_ge(sem("pool_steps"), 1)
            pool.affine_select(out=ident[:, :], in_=ident[:, :], compare_op=ALU.not_equal, fill=1.0, base=0,
                               pattern=[[-1, P]], channel_multiplier=1).then_inc(sem("ident_made"), 1)
            pool.memset(u[:, :, :], 0.0).then_inc(sem("u_zero"), 1)

            def fetch_gate(layer, which):
                for cond in range(2):
                    pool.dma_start(gate[:, cond, :], gates_dram[layer, cond, which].partition_broadcast(P))\
                        .then_inc(sem("gate_in"), 16)

            pool.wait_ge(sem("gates_out0"), 16)
            fetch_gate(0, 0)
            pool.wait_ge(chunk_used, ADA1)
            pool.dma_start(mrow[4:5, :], d["ada_b"][1:2, :]).then_inc(sem("bias_in1"), 16)
            pool.wait_ge(lo_made, ADA1)
            with pool.Fori(0, 4) as it:
                for k in range(6):
                    make_lo(pool, ADA1 + k, (it, 6))
            pool.wait_ge(sem("conv_x"), TC)
            fetch_gate(0, 1)
            pool.wait_ge(sem("ffn_x"), TC)
            for i in range(2):
                pool.dma_start(tk[:, i, :, :], d["rope_tab"][i].rearrange("(c p) r -> p c r", p=P)).then_inc(sem("tk_in"), 16)
            pool.dma_start(gb[:, 0:RD], d["mla_q_qk_g"][0, P:QKD].partition_broadcast(P)).then_inc(sem("tk_in"), 16)
            pool.dma_start(gb[:, RD:2 * RD], d["mla_k_qk_g"][0, P:QKD].partition_broadcast(P)).then_inc(sem("tk_in"), 16)
            pool.dma_start(gb[:, 2 * RD:2 * RD + KVR], d["mla_kv_norm_g"][0].partition_broadcast(P)).then_inc(sem("tk_in"), 16)
            pool.wait_ge(sem("mla_h_lo"), DK)
            pool.dma_start(ckv[:, KC - 1, 0:KVR], d["cache_ckv"][0, 0]).then_inc(sem("cache_in"), 16)
            pool.dma_start(ckv[:, KC - 1, KVR:KVR + RD], d["cache_krope"][0, 0]).then_inc(sem("cache_in"), 16)
            pool.wait_ge(chunk_used, MLA + 4)
            for i in range(2):
                for h in range(2):
                    dst = tq[:, i, :, :].rearrange("p (c h) r -> p c h r", h=2)[:, :, h, :]
                    pool.dma_start(dst, d["rope_tab"][i, 0:T, :].rearrange("(c p) r -> p c r", p=P)).then_inc(sem("tq_in"), 16)
            pool.wait_ge(sem("ckv_made"), TC)
            pool.dma_start(out["new_ckv"][0, 0], ckv[:, 0, 0:KVR]).then_inc(sem("kv_out"), 16)
            pool.dma_start(out["new_krope"][0, 0], ckv[:, 0, KVR:KVR + RD]).then_inc(sem("kv_out"), 16)
            pool.wait_ge(sem("kv_out"), 32)
            pool.wait_ge(sem("lat_split"), 4)
            pool.wait_ge(sem("kr_ready"), 1)
            pool.memset(yacc[:, :, :], 0.0).then_inc(sem("yacc_zero"), 1)
            pool.wait_ge(sem("att_y"), 2 * NGRP + 1)
            pool.wait_ge(sem("gates_out1"), 16)
            fetch_gate(1, 0)
            pool.dma_start(router[:, :, :], d["moe_router"][0].rearrange("(k p) e -> p k e", p=P)).then_inc(sem("router_in"), 16)
            pool.memset(before[:, :], 1.0).then_inc(sem("moe_const"), 1)
            pool.iota(iota[:, :], pattern=[[1, P]], base=0, channel_multiplier=0,
                      allow_small_or_imprecise_dtypes=True).then_inc(sem("moe_const"), 1)
            pool.memset(G[:, :, 0:1], 0.0).then_inc(sem("moe_const"), 1)
            pool.memset(yh[:, :].bitcast(F32), 0.0).then_inc(sem("moe_const"), 1)
            pool.memset(yl[:, :].bitcast(F32), 0.0).then_inc(sem("moe_const"), 1)
            pool.memset(selT[:, :].bitcast(F32), 0.0).then_inc(sem("moe_const"), 1)
            pool.wait_ge(sem("moe_const"), 6)
            pool.affine_select(out=before[:, :], in_=before[:, :], compare_op=ALU.is_gt, fill=0.0, base=0,
                               pattern=[[1, P]], channel_multiplier=-1).then_inc(sem("moe_const"), 1)
            pool.wait_ge(sem("mla_x"), TC)
            fetch_gate(1, 1)
            pool.wait_ge(sem("logits_made"), 1)
            pool.memset(yacc[:, :, :], 0.0).then_inc(sem("yacc_zero"), 1)
            pool.wait_ge(sem("gate_in"), 8 * 16)

        @block.scalar
        def _(act):
            act.dma_start(x[:, 0, :], d["x_prompt"][0]).then_inc(sem("x_in"), 16)
            act.dma_start(x[:, 1:3, :], d["x_sample"][0].rearrange("(c p) n -> p c n", p=P)).then_inc(sem("x_in"), 16)
            def vrow(n, src):
                k = src.shape[0]
                act.dma_start(vec[n:n + k, 0, :], src).then_inc(sem("vec_in"), 16)
            vrow(CND, d["c"][0].rearrange("(k p) -> k p", p=P))
            vrow(CND + DK, d["c_ctx"].rearrange("(k p) -> k p", p=P))
            for n, name in ((N1G, "norm1_g"), (N2G, "norm2_g"), (DWB, "conv_dw_b"), (LNG, "conv_ln_g"), (LNB, "conv_ln_b"),
                            (QNG, "mla_q_norm_g"), (QNG + 4, "mla_kv_norm_g")):
                vrow(n, d[name].rearrange("a (k p) -> (a k) p", p=P))
            vrow(QKG, d["mla_q_qk_g"][0:1, 0:P])
            vrow(KKG, d["mla_k_qk_g"][0:1, 0:P])
            taps = d["conv_dw"][0].rearrange("w (k p) -> (w k) p", p=P)
            act.dma_start(vec[:, 1, :], taps[0:P, :]).then_inc(sem("vec_in"), 16)
            act.dma_start(vec[0:CW * DK - P, 2, :], taps[P:CW * DK, :]).then_inc(sem("vec_in"), 16)
            act.dma_start(comb[:, :], d["comb_tab"]).then_inc(sem("vec_in"), 16)
            act.dma_start(mrow[4:5, :], d["ada_b"][0:1, :]).then_inc(sem("bias_in0"), 16)

            def ada_rows(layer, base):
                act.sem_inc(sem(f"ada_row{layer}"), 3)
                with act.Fori(0, 4) as it:
                    for k in range(6):
                        if k % 2:
                            act.wait_ge(chunk_used, at(base + k + 1, (it, 6)))
                            act.activation(mrow[0:4, ds(it * 1536 + 512 * (k // 2), 512)], ps[0:4, k // 2, :],
                                           ACT.Copy).then_inc(sem(f"ada_row{layer}"), 1)
                        make_hi(act, base + k + 3, (it, 6))

            def ada_gates(layer):
                act.wait_ge(sem(f"gate_rows{layer}"), 1)
                if layer:
                    act.wait_ge(sem("gates_out0"), 16)
                act.activation(grow[:, :, :], ps[0:2, 4:8, :], ACT.Copy).then_inc(sem(f"grow_made{layer}"), 1)
                act.wait_ge(sem(f"grow_made{layer}"), 1)
                act.dma_start(gates_dram[layer].rearrange("c w n -> c (w n)"), grow[:, :, :].rearrange("c k n -> c (k n)"))\
                    .then_inc(sem(f"gates_out{layer}"), 16)

            for s in range(3):
                make_hi(act, s)
            act.wait_ge(sem("vT_made"), 1)
            act.activation(st[:, 16:32], vT[:, CND:CND + 16], ACT.Silu).then_inc(sem("cond_made"), 1)
            ada_rows(0, 0)
            ada_gates(0)
            norm_act(act, "conv", 0, 0, "x_in", 32)
            for t in range(4):
                make_hi(act, PW1 + 2 * t + 3)
                act.wait_ge(chunk_used, PW1 + 2 * t + 2)
                if t >= 2:
                    act.wait_ge(sem("glu_done"), 2 * (t - 1))
                b = 4 * (t % 2) + 2
                act.activation(sig[:, t % 2, :, :], ps[:, b:b + 2, 0:T], ACT.Sigmoid).then_inc(sem("sig_made"), 1)
                if t < 3:
                    make_hi(act, PW1 + 2 * t + 4)
            make_hi(act, ADA1 + 2)
            ada_rows(1, ADA1)
            ada_gates(1)
            for j in range(DK):
                act.wait_ge(sem("ln_centred"), j + 1)
                if j >= 2:
                    act.wait_ge(sem("ln_summed"), j - 1)
                act.activation(sq[:, j % 2, :], v[:, j, :], ACT.Square).then_inc(sem("ln_square"), 1)
            act.wait_ge(sem("ln_summed"), DK)
            act.activation(sd[:, :], ps[:, 1, 0:CV], ACT.Sqrt, scale=1.0 / D, bias=epsc[:, 0:1]).then_inc(sem("ln_root"), 1)
            for j in range(DK):
                act.wait_ge(sem("ln_scaled"), j + 1)
                for a, b, o in ((0, P, 0), (P, T, SV - P)):
                    act.activation(hf[:, j, a:b], v[:, j, a + o:b + o], ACT.Silu, scale=vT[:, LNG + j:LNG + j + 1],
                                   bias=vT[:, LNB + j:LNB + j + 1]).then_inc(sem("ln_done"), 1)
            for q in range(DK // 2):
                make_hi(act, PW2 + q + 3)
            norm_act(act, "ffn", 0, 1, "conv_x", TC)
            act.wait_ge(sem("gates_out1"), 16)

            def gate_silu(b, value, loop, free=True):
                if free:
                    act.wait_ge(sem("ffn_prod"), at(value - 2, loop))
                act.activation(fs[:, b, :], ps[:, 6, 0:T], ACT.Silu).then_inc(sem("ffn_silu"), 1)

            act.wait_ge(sem("ffn_up"), 1)
            gate_silu(0, 1, None, False)
            act.wait_ge(chunk_used, FFN + 1)
            gate_silu(1, 2, None, False)
            make_hi(act, FFN + 3)
            make_hi(act, FFN + 4)
            act.wait_ge(sem("ffn_up"), 3)
            gate_silu(0, 3, None)
            make_hi(act, FFN + 5)
            with act.Fori(0, 4) as it:
                for i in (1, 2):
                    act.wait_ge(chunk_used, at(FFN + 3 * i + 1, (it, 6)))
                    gate_silu(1, 2 * i + 2, (it, 4))
                    make_hi(act, FFN + 3 * i + 3, (it, 6))
                    make_hi(act, FFN + 3 * i + 4, (it, 6))
                    act.wait_ge(sem("ffn_up"), at(2 * i + 3, (it, 4)))
                    gate_silu(0, 2 * i + 3, (it, 4))
                    make_hi(act, FFN + 3 * i + 5, (it, 6))
            act.wait_ge(chunk_used, FFN + 28)
            gate_silu(1, 20, None)
            make_hi(act, FFN + 30)
            make_hi(act, FFN + 31)
            act.wait_ge(sem("ffn_up"), 21)
            gate_silu(0, 21, None)
            make_hi(act, FFN + 32)
            act.wait_ge(chunk_used, FFN + 31)
            gate_silu(1, 22, None)
            for i in range(3):
                make_hi(act, MLA + i)
            norm_act(act, "mla", 1, 0, "ffn_x", TC)
            make_hi(act, MLA + 3)
            act.wait_ge(chunk_used, MLA + 2)
            for c in range(TC):
                act.activation(q_sb[:, 0:3, 0:QKD].rearrange("p a b -> p (a b)")[:, 0:QLR] if c == 0 else KT[:, c - 1, :],
                               ps[:, c, :], ACT.Square, scale=QLR ** -0.5,
                               accum_out=st[:, c:c + 1]).then_inc(sem("lat_squares"), 1)
            make_hi(act, MLA + 4)
            make_hi(act, MLA + 5)
            act.wait_ge(chunk_used, MLA + 4)
            for c in range(TC):
                act.activation(QB[:, c, 0:KVR], ps[:, 3 + c, 0:KVR], ACT.Square, scale=KVR ** -0.5,
                               accum_out=st[:, 3 + c:4 + c]).then_inc(sem("lat_squares"), 1)
            make_hi(act, MLA + 6)
            for k in range(4):
                act.wait_ge(sem("cq_turned"), k + 1)
                act.activation(cqf[:, k, :], ps[:, 6 + k % 2, 0:T], ACT.Copy,
                               scale=vT[:, QNG + k:QNG + k + 1]).then_inc(sem("cq_scaled"), 1)
            act.wait_ge(sem("ckv_made"), TC)
            act.wait_ge(sem("cache_in"), 32)
            act.activation(pT[:, 0:KC * RD].rearrange("p (c r) -> p c r", c=KC), ckv[:, :, KVR:KVR + RD], ACT.Square)\
                .then_inc(sem("kr_square"), 1)

            with act.Fori(0, NGRP) as g:
                for i in range(2):
                    kv, q = GRP + 2 * i, GRP + 2 * i + 1
                    n = i + 1
                    pair = (g, 2)
                    act.wait_ge(chunk_used, at(kv + 1, (g, 6)))
                    act.activation(kv_sb[:, :, :], ps[:, 0:4, :], ACT.Copy).then_inc(sem("k_copied"), 1)
                    act.activation(KT[:, :, :].rearrange("p a b -> p (a b)").rearrange("p (c h r) -> p c h r", c=KC, h=2),
                                   ps[:, 0:4, :].rearrange("p c (h r) -> p c h r", h=2)[:, :, :, 0:P],
                                   ACT.Square).then_inc(sem("k_square"), 1)
                    make_hi(act, kv + 3, (g, 6))
                    act.wait_ge(chunk_used, at(q + 1, (g, 6)))
                    act.activation(q_sb[:, :, :].rearrange("p a r -> p (a r)").rearrange("p (c n) -> p c n", c=TC),
                                   ps[:, 4:7, 0:384], ACT.Copy).then_inc(sem("q_copied"), 1)
                    act.activation(QB[:, :, :], ps[:, 4:7, 0:384], ACT.Square).then_inc(sem("q_square"), 1)
                    make_hi(act, q + 3, (g, 6))
                    act.wait_ge(sem("k_turned"), at(n, pair))
                    act.activation(KT[:, :, :], ps[:, 0:2, :], ACT.Copy, scale=vT[:, KKG:KKG + 1]).then_inc(sem("kT_made"), 1)
                    act.wait_ge(sem("q_turned"), at(n, pair))
                    for h in range(2):
                        act.activation(QB[:, h, :], ps[:, 3 + 4 * h, 0:T], ACT.Copy,
                                       scale=vT[:, QKG:QKG + 1]).then_inc(sem("kT_made"), 1)
                    for h in range(2):
                        for c in range(TC):
                            act.wait_ge(sem("max_made"), at(6 * i + 3 * h + max(c, 1) + 1, (g, 12)))
                            a, b = ((0, P), (P, 4 * P), (0, 3 * P))[c]
                            o = (0, P, 4 * P)[c]
                            act.activation(pr[:, h, o:o + b - a], ps[:, 2 * h + c // 2, a:b], ACT.Exp,
                                           bias=st[:, 40 + 3 * h + c:41 + 3 * h + c],
                                           accum_out=st[:, 48 + 3 * h + c:49 + 3 * h + c]).then_inc(sem("exp_made"), 1)
                    for h in range(2):
                        act.wait_ge(sem("p_turned"), at(2 * i + h + 1, (g, 4)))
                        act.activation(pT[:, 0:512], ps[:, 4, :], ACT.Copy).then_inc(sem("pT_hi"), 1)
                        act.wait_ge(sem("o_made"), at(2 * i + h + 1, (g, 4)))
                        act.activation(oTh[:, 2 * i + h, :], ps[:, 6 + h, 0:T], ACT.Copy).then_inc(sem("oT_hi"), 1)
                for i in range(2):
                    make_hi(act, GRP + 4 + i + 3, (g, 6))

            norm_act(act, "moe", 1, 1, "mla_x", TC)
            act.wait_ge(sem("tok_turned"), 1)
            for c in range(TC):
                act.activation(xn[:, c, :], ps[:, 2 * c:2 * c + 2, :].rearrange("p a b -> p (a b)"), ACT.Copy)\
                    .then_inc(sem("tok_made"), 1)
            act.wait_ge(sem("gap_made"), 1)
            act.activation(rt[:, 9, :, 1:2], rt[:, 9, :, 0:1], ACT.Exp).then_inc(sem("gap_exp"), 1)

            def heads(t):
                for k in range(3):
                    make_hi(act, MOE + k, (t, TILE_CH))

            def tile(t):
                L = (t, TILE_CH)
                act.wait_ge(sem("gathered"), at(1, (t, 1)))
                act.activation(xgh[:, :, :].rearrange("p a b -> p (a b)"), ps[:, 4:6, :].rearrange("p a b -> p (a b)"),
                               ACT.Copy).then_inc(sem("xg_hi"), 1)
                for k in range(14 + 1):
                    if k in (1, 5, 9):
                        g = k // 4
                        act.wait_ge(chunk_used, at(MOE + k + 1, L))
                        act.wait_ge(sem("hm_made"), at(g + 1, (t, 3)))
                        act.activation(ms[:, :], ps[:, 2 * (g % 2), :], ACT.Silu).then_inc(sem("ms_made"), 1)
                    if k in (5, 9, 13):
                        g = k // 4 - 1
                        act.wait_ge(sem("hm_turned"), at(g + 1, (t, 3)))
                        act.activation(hgh[:, 4 * g:4 * g + 4, :].rearrange("p a b -> p (a b)"), ps[:, 5 - g % 2, :],
                                       ACT.Copy).then_inc(sem("hg_hi"), 1)
                    make_hi(act, MOE + k + 3, L)
                    if k == 0:
                        act.wait_ge(sem("sel_turned"), at(1, (t, 1)))
                        act.activation(selT[:, :], ps[:, 4, 0:T], ACT.Copy).then_inc(sem("selT_made"), 1)
                act.wait_ge(chunk_used, at(MOE + TILE_CH, L))
                act.activation(yh[:, :], ps[:, 6:8, :].rearrange("p a b -> p (a b)"), ACT.Copy).then_inc(sem("y_hi"), 1)

            act.wait_ge(sem("moe_const"), 7)
            with act.Fori(0, NE - 1) as e:
                tile(e)
                heads(e + 1)
            tile(NE - 1)
            act.wait_ge(sem("tab_ready"), 1)
            more = act.value_load(tab[0:1, 0:1], min_val=0, max_val=NX)
            with act.Fori(0, NX) as j:
                with act.If(j < more):
                    heads(j + NE)
                    tile(j + NE)

        @block.vector
        def _(dve):
            step = Steps(dve, sem("dve_steps"))
            dve.wait_ge(sem("ident_made"), 1)
            dve.wait_ge(sem("vec_turned"), 1)
            dve.tensor_copy(dwT[:, 0:P], ps[:, 7, P:2 * P]).then_inc(sem("dw_made"), 1)
            dve.tensor_copy(dwT[:, P:CW * DK], ps[:, 7, 2 * P:P + CW * DK]).then_inc(sem("dw_made"), 1)
            dve.tensor_copy(vT[:, :], ps[:, 7, 0:80]).then_inc(sem("vT_made"), 1)
            dve.wait_ge(sem("cond_made"), 1)
            dve.wait_ge(sem("cst_zero"), 1)
            cnd = st[:, 16:32].rearrange("p (s k) -> p k s", k=DK)
            step(dve.tensor_copy(cst[:, :, 0:2], cnd))
            dve.tensor_tensor(cst[:, :, 2:4], cnd, cst[:, :, 0:2], ALU.subtract).then_inc(sem("cst_made"), 1)

            def modulation(layer):
                dve.wait_ge(sem(f"rows_turned{layer}"), 1)
                step(dve.tensor_copy(mT[:, :, :], ps[:, 3, 0:256].rearrange("p (m r) -> p m r", r=8)[:, :, 0:5]))
                for cond in range(2):
                    m = modv[:, layer, cond, :, :].rearrange("p a b -> p (a b)")
                    step(dve.tensor_tensor(m, mT[:, :, cond], mT[:, :, cond + 2], ALU.add))
                    step(dve.tensor_tensor(m, m, mT[:, :, 4], ALU.add))
                for n, g0 in ((0, N1G), (1, N2G)):
                    for cond in range(2):
                        step(dve.scalar_tensor_tensor(
                            out=modA[:, layer, n, cond, :], in0=modv[:, layer, cond, 2 * n + 1, :], scalar=1.0,
                            in1=vT[:, g0 + DK * layer:g0 + DK * layer + DK], op0=ALU.add, op1=ALU.mult))
                dve.tensor_copy(st[:, 63:64], ones[:, 0:1]).then_inc(sem(f"mod_ready{layer}"), 1)

            for s in range(3):
                make_lo(dve, s)
            with dve.Fori(0, 4) as it:
                for k in range(6):
                    make_lo(dve, k + 3, (it, 6))
            dve.wait_ge(sem("ones_made"), 2)
            modulation(0)
            norm_dve(dve, step, "conv")
            split_dve(dve, "conv", "conv_modulated", 2)
            dve.wait_ge(sem("u_zero"), 1)
            for t in range(4):
                if t < 3:
                    make_lo(dve, PW1 + 2 * t + 3)
                dve.wait_ge(sem("sig_made"), t + 1)
                b = 4 * (t % 2)
                for a, e, o in ((0, P, PAD), (P, T, 2 * PAD)):
                    dve.tensor_tensor(u[:, 2 * t:2 * t + 2, a + o:e + o], ps[:, b:b + 2, a:e], sig[:, t % 2, :, a:e],
                                      ALU.mult).then_inc(sem("glu_done"), 1)
                if t < 3 and 2 * t + 4 < 8:
                    make_lo(dve, PW1 + 2 * t + 4)
            dve.wait_ge(sem("glu_done"), 8)
            dve.wait_ge(sem("dw_made"), 2)
            with dve.Fori(0, 4) as it:
                step.begin(it, 2 * (CW - 1))
                for i in range(2):
                    j = it * 2 + i
                    vj = v[:, ds(j, 1), :].rearrange("p a b -> p (a b)")
                    step(dve.tensor_scalar(vj, u[:, ds(j, 1), 0:CV].rearrange("p a b -> p (a b)"), dwT[:, ds(j, 1)],
                                           vT[:, ds(j + DWB, 1)], ALU.mult, ALU.add))
                    for w in range(1, CW):
                        ins = dve.scalar_tensor_tensor(
                            out=vj, in0=u[:, ds(j, 1), w:w + CV].rearrange("p a b -> p (a b)"),
                            scalar=dwT[:, ds(j + w * DK, 1)], in1=vj, op0=ALU.mult, op1=ALU.add)
                        if w < CW - 1:
                            step(ins)
                        else:
                            ins.then_inc(sem("conv_done"), 1)
                step.end(4)
            modulation(1)
            dve.wait_ge(sem("ln_mean"), 1)
            dve.wait_ge(sem("conv_done"), DK)
            for j in range(DK):
                dve.scalar_tensor_tensor(out=v[:, j, :], in0=ps[:, 0, 0:CV], scalar=-1.0 / D, in1=v[:, j, :],
                                         op0=ALU.mult, op1=ALU.add).then_inc(sem("ln_centred"), 1)
            dve.wait_ge(lo_made, PW2)
            for s in range(3):
                make_lo(dve, PW2 + s)
            dve.wait_ge(sem("ln_root"), 1)
            step(dve.reciprocal(rs[:, :], sd[:, :]))
            dve.wait_ge(sem("ln_centred"), DK)
            for j in range(DK):
                dve.tensor_tensor(v[:, j, :], v[:, j, :], rs[:, :], ALU.mult).then_inc(sem("ln_scaled"), 1)
            split_dve(dve, "ln", "ln_done", 2)
            for q in range(DK // 2):
                make_lo(dve, PW2 + q + 3)
            dve.wait_ge(chunk_used, PW2 + 4)
            dve.wait_ge(sem("gate_in"), 32)
            residual(dve, step, "conv", lambda c: ps[:, 2 * c:2 * c + 2, :].rearrange("p a b -> p (a b)"))

            norm_dve(dve, step, "ffn")
            dve.wait_ge(sem("gates_out1"), 16)
            split_dve(dve, "ffn", "ffn_modulated", 2)

            def hidden(b, value, loop, up, free):
                dve.wait_ge(sem("ffn_silu"), at(value, loop))
                dve.wait_ge(*up)
                if free:
                    dve.wait_ge(*free)
                dve.tensor_tensor(ff[:, b, :], ps[:, 7, 0:T], fs[:, b, :], ALU.mult).then_inc(sem("ffn_prod"), 1)
                dve.wait_ge(sem("ffn_prod"), at(value, loop))
                dve.tensor_copy(fh[:, b, :], ff[:, b, :]).then_inc(sem("ffn_hi"), 1)
                dve.wait_ge(sem("ffn_hi"), at(value, loop))
                dve.tensor_tensor(fl[:, b, :], ff[:, b, :], fh[:, b, :], ALU.subtract).then_inc(sem("ffn_lo"), 1)

            up, down = sem("ffn_up"), sem("ffn_down")
            hidden(0, 1, None, (up, 2), None)
            hidden(1, 2, None, (chunk_used, FFN + 2), None)
            make_lo(dve, FFN + 3)
            make_lo(dve, FFN + 4)
            hidden(0, 3, None, (up, 4), (down, 1))
            make_lo(dve, FFN + 5)
            with dve.Fori(0, 4) as it:
                for i in (1, 2):
                    hidden(1, 2 * i + 2, (it, 4), (chunk_used, at(FFN + 3 * i + 2, (it, 6))), None)
                    make_lo(dve, FFN + 3 * i + 3, (it, 6))
                    make_lo(dve, FFN + 3 * i + 4, (it, 6))
                    hidden(0, 2 * i + 3, (it, 4), (up, at(2 * i + 4, (it, 4))), (down, at(i + 1, (it, 2))))
                    make_lo(dve, FFN + 3 * i + 5, (it, 6))
            hidden(1, 20, None, (chunk_used, FFN + 29), None)
            make_lo(dve, FFN + 30)
            make_lo(dve, FFN + 31)
            hidden(0, 21, None, (up, 22), (down, 10))
            make_lo(dve, FFN + 32)
            hidden(1, 22, None, (chunk_used, FFN + 32), None)
            for i in range(3):
                make_lo(dve, MLA + i)
            dve.wait_ge(chunk_used, FFN + 33)
            dve.wait_ge(sem("gate_in"), 64)
            residual(dve, step, "ffn", lambda c: ps[:, 2 * c:2 * c + 2, :].rearrange("p a b -> p (a b)"))

            norm_dve(dve, step, "mla")
            split_dve(dve, "mla", "mla_modulated", 2)
            make_lo(dve, MLA + 3)
            dve.wait_ge(sem("lat_squares"), TC)
            rsqrt(step, st[:, 6:9], st[:, 0:3], TC)
            for c in range(TC):
                dve.tensor_scalar(xn[:, c, 0:QLR], ps[:, c, :], st[:, 6 + c:7 + c], None, ALU.mult).then_inc(sem("cq_made"), 1)
            make_lo(dve, MLA + 4)
            make_lo(dve, MLA + 5)
            dve.wait_ge(sem("lat_squares"), 2 * TC)
            rsqrt(step, st[:, 9:12], st[:, 3:6], TC)
            for c in range(TC):
                step(dve.tensor_copy(ckv[:, c, KVR:KVR + RD], ps[:, 3 + c, KVR:KVR + RD]))
                step(dve.tensor_scalar(ckv[:, c, 0:KVR], ps[:, 3 + c, 0:KVR], st[:, 9 + c:10 + c], None, ALU.mult))
            dve.wait_ge(sem("tk_in"), 5 * 16)
            for c in range(TC):
                dve.tensor_tensor(ckv[:, c, 0:KVR], ckv[:, c, 0:KVR], gb[:, 2 * RD:2 * RD + KVR],
                                  ALU.mult).then_inc(sem("ckv_made"), 1)
            make_lo(dve, MLA + 6)
            dve.wait_ge(sem("tq_in"), 4 * 16)

            def by_half(t):
                w = t.rearrange("p n (a h r) -> p n a h r", a=2, h=2)
                return w[:, :, :, 0, :], w[:, :, :, 1, :]

            for tab_, g0, n in ((tk, RD, KC), (tq, 0, 2 * TC)):
                g = gb[:, g0:g0 + RD]
                step(dve.tensor_tensor(tab_[:, 0, :, :], tab_[:, 0, :, :], g.unsqueeze(1).to_broadcast([P, n, RD]), ALU.mult))
                s = by_half(tab_[:, 1, :, :])
                gh = by_half(g.unsqueeze(1).to_broadcast([P, n, RD]))
                for h in range(2):
                    step(dve.tensor_tensor(s[h], s[h], gh[1 - h], ALU.mult))

            def rotate(dst, tmp, src, tab_):
                step(dve.tensor_tensor(dst, src, tab_[:, 0, :, :], ALU.mult))
                a, b, s = by_half(tmp), by_half(src), by_half(tab_[:, 1, :, :])
                for h in range(2):
                    step(dve.tensor_tensor(a[h], b[1 - h], s[h], ALU.mult))

            dve.wait_ge(sem("ckv_made"), TC)
            dve.wait_ge(sem("cache_in"), 32)
            dve.wait_ge(sem("kr_square"), 1)
            step(dve.tensor_reduce(st[:, 12:16], pT[:, 0:KC * RD].rearrange("p (c r) -> p c r", c=KC), AX, ALU.add))
            qrt = qr[:, 0, 0:KC, :]
            rotate(kr_rot[:, :, :], qrt, ckv[:, :, KVR:KVR + RD], tk)
            dve.tensor_tensor(kr_rot[:, :, :], kr_rot[:, :, :], qrt, ALU.add).then_inc(sem("kr_ready"), 1)
            for k in range(4):
                dve.wait_ge(sem("cq_scaled"), k + 1)
                step(dve.tensor_copy(cqTh[:, k, :], cqf[:, k, :]))
                step(dve.tensor_tensor(cqTl[:, k, :], cqf[:, k, :], cqTh[:, k, :], ALU.subtract))
            for k in range(2):
                dve.wait_ge(sem("ck_turned"), k + 1)
                dve.tensor_copy(ckTh[:, k, :], ps[:, k, :]).then_inc(sem("lat_split"), 1)
                dve.wait_ge(sem("lat_split"), 2 * k + 1)
                dve.tensor_tensor(ckTl[:, k, :], ps[:, k, :], ckTh[:, k, :], ALU.subtract).then_inc(sem("lat_split"), 1)
            dve.wait_ge(sem("yacc_zero"), 1)
            dve.sem_inc(sem("att_y"), 1)

            with dve.Fori(0, NGRP) as g:
                step.begin(g, 2 * (2 * RSQRT_STEPS + 13))
                for i in range(2):
                    kv, q = GRP + 2 * i, GRP + 2 * i + 1
                    n, pair = i + 1, (g, 2)
                    dve.wait_ge(sem("k_square"), at(n, pair))
                    step(dve.tensor_reduce(st[:, 16:24], KT[:, :, :].rearrange("p a b -> p (a b)")
                                           .rearrange("p (c r) -> p c r", r=P), AX, ALU.add))
                    step(dve.tensor_tensor(st[:, 16:24].rearrange("p (c h) -> p c h", h=2),
                                           st[:, 16:24].rearrange("p (c h) -> p c h", h=2),
                                           st[:, 12:16].unsqueeze(2).to_broadcast([P, KC, 2]), ALU.add))
                    step(dve.tensor_scalar(st[:, 16:24], st[:, 16:24], 1.0 / QKD, None, ALU.mult))
                    rsqrt(step, st[:, 24:32], st[:, 16:24], 8)
                    dve.wait_ge(sem("k_copied"), at(n, pair))
                    rk = st[:, 24:32].rearrange("p (c h) -> p c h", h=2)
                    kk = kv_sb[:, :, :].rearrange("p c (h r) -> p c h r", h=2)[:, :, :, 0:P]
                    step(dve.tensor_tensor(kk, kk, rk.unsqueeze(3).to_broadcast([P, KC, 2, P]), ALU.mult))
                    dve.tensor_tensor(krh[:, :, :, :], kr_rot[:, :, :].unsqueeze(2).to_broadcast([P, KC, 2, RD]),
                                      rk.unsqueeze(3).to_broadcast([P, KC, 2, RD]), ALU.mult).then_inc(sem("k_scaled"), 1)
                    make_lo(dve, kv + 3, (g, 6))
                    dve.wait_ge(sem("q_square"), at(n, pair))
                    step(dve.tensor_reduce(st[:, 32:38], QB[:, :, :].rearrange("p a b -> p (a b)")
                                           .rearrange("p (c r) -> p c r", r=QKD), AX, ALU.add))
                    step(dve.tensor_scalar(st[:, 32:38], st[:, 32:38], 1.0 / QKD, None, ALU.mult))
                    rsqrt(step, st[:, 56:62], st[:, 32:38], 6)
                    step(dve.tensor_scalar(st[:, 56:62], st[:, 56:62], QKD ** -0.5, None, ALU.mult))
                    dve.wait_ge(sem("q_copied"), at(n, pair))
                    step(dve.tensor_tensor(q_sb[:, :, :], q_sb[:, :, :],
                                           st[:, 56:62].unsqueeze(2).to_broadcast([P, 2 * TC, QKD]), ALU.mult))
                    rotate(qr[:, 0, :, :], qr[:, 1, :, :], q_sb[:, :, P:QKD], tq)
                    dve.tensor_tensor(qr[:, 0, :, :], qr[:, 0, :, :], qr[:, 1, :, :], ALU.add).then_inc(sem("q_scaled"), 1)
                    make_lo(dve, q + 3, (g, 6))
                    dve.wait_ge(sem("k_turned"), at(n, pair))
                    dve.tensor_copy(KR[:, :], ps[:, 2, :]).then_inc(sem("rT_made"), 1)
                    dve.wait_ge(sem("q_turned"), at(n, pair))
                    dve.tensor_copy(QB[:, 2, :], ps[:, 4, 0:T]).then_inc(sem("rT_made"), 1)
                    for h in range(2):
                        dve.wait_ge(sem("scored"), at(2 * i + h + 1, (g, 4)))
                        for c in range(TC):
                            a, b = ((0, P), (P, 4 * P), (0, 3 * P))[c]
                            dve.tensor_reduce(st[:, 40 + 3 * h + c:41 + 3 * h + c], ps[:, 2 * h + c // 2, a:b], AX, ALU.max,
                                              negate=True).then_inc(sem("max_made"), 1)
                    for h in range(2):
                        dve.wait_ge(sem("exp_made"), at(6 * i + 3 * h + 3, (g, 12)))
                        step(dve.reciprocal(st[:, 3 * h:3 * h + 3], st[:, 48 + 3 * h:51 + 3 * h]))
                        for c in range(TC):
                            o, e = ((0, P), (P, 4 * P), (4 * P, 7 * P))[c]
                            dve.tensor_scalar(pr[:, h, o:e], pr[:, h, o:e], st[:, 3 * h + c:3 * h + c + 1], None,
                                              ALU.mult).then_inc(sem("p_made"), 1)
                    for h in range(2):
                        dve.wait_ge(sem("p_turned"), at(2 * i + h + 1, (g, 4)))
                        dve.tensor_copy(pT[:, 512:7 * P], ps[:, 5, 0:T]).then_inc(sem("pT_lo"), 1)
                        dve.wait_ge(sem("oT_hi"), at(2 * i + h + 1, (g, 4)))
                        dve.tensor_tensor(oTl[:, 2 * i + h, :], ps[:, 6 + h, 0:T], oTh[:, 2 * i + h, :],
                                          ALU.subtract).then_inc(sem("oT_lo"), 1)
                for i in range(2):
                    make_lo(dve, GRP + 4 + i + 3, (g, 6))
                    dve.wait_ge(chunk_used, at(GRP + 4 + i + 1, (g, 6)))
                    ya = yacc[:, :, i * 512:i * 512 + 512]
                    dve.wait_ge(sem("att_y"), at(i + 1, (g, 2)))
                    dve.tensor_tensor(ya, ya, ps[:, 3 * i:3 * i + 3, :], ALU.add).then_inc(sem("att_y"), 1)
                step.end(NGRP)
            dve.wait_ge(sem("att_y"), 2 * NGRP + 1)
            dve.wait_ge(sem("gate_in"), 96)
            residual(dve, step, "mla", lambda c: yacc[:, c, :])

            norm_dve(dve, step, "moe")
            dve.wait_ge(sem("moe_const"), 7)
            dve.wait_ge(sem("logits_made"), 1)
            L, W, O1, O2, L2, GT, M, TMP = (rt[:, i, :, :] for i in range(8))
            stt = rt[:, 8, :, :]
            gap = rt[:, 9, :, :]
            rev = rt[:, 10, :, :]
            wide = [P, TC, NE]

            def one(t, i):
                return t[:, :, i:i + 1].to_broadcast(wide)

            step(dve.tensor_copy(L, ps[:, 6, 0:TC * NE].rearrange("p (c e) -> p c e", c=TC)))
            for c in range(TC):
                step(dve.tensor_scalar(rev[:, c, :], iota[:, 0:NE], -1.0, float(NE), ALU.mult, ALU.add))

            def best(src, oh, m):
                step(dve.tensor_reduce(stt[:, :, m:m + 1], src, AX, ALU.max))
                step(dve.tensor_tensor(W, src, one(stt, m), ALU.is_equal))
                step(dve.tensor_tensor(W, W, rev, ALU.mult))
                step(dve.tensor_reduce(stt[:, :, m + 1:m + 2], W, AX, ALU.max))
                step(dve.tensor_tensor(oh, W, one(stt, m + 1), ALU.is_equal))

            best(L, O1, 0)
            step(dve.scalar_tensor_tensor(out=L2, in0=O1, scalar=GONE, in1=L, op0=ALU.mult, op1=ALU.add))
            best(L2, O2, 2)
            step(dve.tensor_tensor(M, O1, O2, ALU.add))
            dve.tensor_tensor(gap[:, :, 0:1], stt[:, :, 2:3], stt[:, :, 0:1], ALU.subtract).then_inc(sem("gap_made"), 1)
            dve.wait_ge(sem("gap_exp"), 1)
            step(dve.tensor_scalar(gap[:, :, 2:3], gap[:, :, 1:2], 1.0, None, ALU.add))
            step(dve.reciprocal(gap[:, :, 3:4], gap[:, :, 2:3]))
            step(dve.tensor_tensor(gap[:, :, 4:5], gap[:, :, 1:2], gap[:, :, 3:4], ALU.mult))
            step(dve.tensor_tensor(GT, O1, one(gap, 3), ALU.mult))
            step(dve.tensor_tensor(TMP, O2, one(gap, 4), ALU.mult))
            step(dve.tensor_tensor(GT, GT, TMP, ALU.add))
            step(dve.tensor_copy(G[:, :, 1:NE + 1], GT))
            dve.wait_ge(sem("ranked"), 1)
            rk = ps[:, 7, 0:TC * NE].rearrange("p (c e) -> p c e", c=TC)
            step(dve.scalar_tensor_tensor(out=TMP, in0=rk, scalar=BIG, in1=M, op0=ALU.add, op1=ALU.mult))
            step(dve.tensor_scalar(R[:, :, 0:NE], TMP, -BIG, None, ALU.add))

            def make_sel(t):
                for c in range(TC):
                    dve.tensor_scalar(sel[:, c, :], iota[:, :], R[:, c, t], None, ALU.is_equal).then_inc(sem("sel_made"), 1)

            make_sel(slice(0, 1))
            cnt, ex, cum, cux, one_, t1 = (jt[:, i, :] for i in range(6))
            step(dve.tensor_copy(cnt, ps[:, 7, TC * NE:TC * NE + NE]))
            step(dve.tensor_scalar(ex, cnt, float(P), None, ALU.is_gt))
            for b in range(2, TC):
                step(dve.scalar_tensor_tensor(out=ex, in0=cnt, scalar=float(b * P), in1=ex, op0=ALU.is_gt, op1=ALU.add))
            step(dve.tensor_copy(cum[:, 0:1], ex[:, 0:1]))
            for e in range(1, NE):
                step(dve.tensor_tensor(cum[:, e:e + 1], cum[:, e - 1:e], ex[:, e:e + 1], ALU.add))
            step(dve.tensor_tensor(cux, cum, ex, ALU.subtract))
            step(dve.memset(R[:, :, NE:NT], -BIG))
            step(dve.memset(G[:, :, NE + 1:NT + 1], 0.0))
            ids = jt[:, 6, :]
            step(dve.tensor_copy(ids[:, 0:1], cum[:, NE - 1:NE]))
            for j in range(NX):
                step(dve.tensor_scalar(one_, cum, float(j), None, ALU.is_gt))
                step(dve.scalar_tensor_tensor(out=one_, in0=cux, scalar=float(j), in1=one_, op0=ALU.is_le, op1=ALU.mult))
                step(dve.tensor_scalar(t1, cux, float(P), float(-P * (j + 1)), ALU.mult, ALU.add))
                ow = one_.unsqueeze(1).to_broadcast(wide)
                step(dve.tensor_tensor(TMP, R[:, :, 0:NE], t1.unsqueeze(1).to_broadcast(wide), ALU.add))
                step(dve.tensor_scalar(TMP, TMP, BIG, None, ALU.add))
                step(dve.tensor_tensor(TMP, TMP, ow, ALU.mult))
                step(dve.tensor_reduce(stt[:, :, 4:5], TMP, AX, ALU.add))
                step(dve.tensor_scalar(R[:, :, NE + j:NE + j + 1], stt[:, :, 4:5], -BIG, None, ALU.add))
                step(dve.tensor_tensor(TMP, GT, ow, ALU.mult))
                step(dve.tensor_reduce(G[:, :, NE + 1 + j:NE + 2 + j], TMP, AX, ALU.add))
                step(dve.tensor_tensor(t1, one_, iota[:, 0:NE], ALU.mult))
                step(dve.tensor_reduce(ids[:, 1 + j:2 + j], t1, AX, ALU.add))
            dve.tensor_copy(tab[0:1, 0:NX + 1], ids[0:1, 0:NX + 1]).then_inc(sem("tab_ready"), 1)
            dve.sem_inc(sem("hm_made"), 1)
            dve.sem_inc(sem("y_lo"), 1)
            dve.wait_ge(sem("yacc_zero"), 2)

            def heads(t):
                for k in range(3):
                    make_lo(dve, MOE + k, (t, TILE_CH))

            def add_scattered(c, t, value):
                b = (0, 2, 6)[c]
                dve.wait_ge(sem("scattered"), value)
                dve.scalar_tensor_tensor(out=yacc[:, c, :], in0=ps[:, b:b + 2, :].rearrange("p a b -> p (a b)"),
                                         scalar=G[:, c, t], in1=yacc[:, c, :], op0=ALU.mult, op1=ALU.add)\
                    .then_inc(sem("y_added"), 1)

            def tile(t):
                L = (t, TILE_CH)
                tt = ds(t, 1)
                dve.wait_ge(sem("xg_hi"), at(1, (t, 1)))
                dve.tensor_tensor(xgl[:, :, :].rearrange("p a b -> p (a b)"), ps[:, 4:6, :].rearrange("p a b -> p (a b)"),
                                  xgh[:, :, :].rearrange("p a b -> p (a b)"), ALU.subtract).then_inc(sem("xg_lo"), 1)
                add_scattered(0, tt, at(1, (t, 3)))
                add_scattered(1, tt, at(2, (t, 3)))
                make_lo(dve, MOE + 3, L)
                add_scattered(2, tt, at(3, (t, 3)))
                for k in range(1, 15):
                    if k in (3, 7, 11):
                        g = k // 4
                        dve.wait_ge(sem("ms_made"), at(g + 1, (t, 3)))
                        dve.wait_ge(chunk_used, at(MOE + k + 1, L))
                        dve.tensor_tensor(hm[:, g % 2, :], ps[:, 2 * (g % 2) + 1, :], ms[:, :], ALU.mult).then_inc(sem("hm_made"), 1)
                    if k in (5, 9, 13):
                        g = k // 4 - 1
                        dve.wait_ge(sem("hg_hi"), at(g + 1, (t, 3)))
                        dve.tensor_tensor(hgl[:, 4 * g:4 * g + 4, :].rearrange("p a b -> p (a b)"), ps[:, 5 - g % 2, :],
                                          hgh[:, 4 * g:4 * g + 4, :].rearrange("p a b -> p (a b)"),
                                          ALU.subtract).then_inc(sem("hg_lo"), 1)
                    make_lo(dve, MOE + k + 3, L)
                    if k == 8:
                        dve.wait_ge(sem("sel_turned"), at(1, (t, 1)))
                        make_sel(ds(t + 1, 1))
                dve.wait_ge(sem("y_hi"), at(1, (t, 1)))
                dve.tensor_tensor(yl[:, :], ps[:, 6:8, :].rearrange("p a b -> p (a b)"), yh[:, :],
                                  ALU.subtract).then_inc(sem("y_lo"), 1)

            with dve.Fori(0, NE - 1) as e:
                tile(e)
                heads(e + 1)
            tile(NE - 1)
            more = dve.value_load(tab[0:1, 0:1], min_val=0, max_val=NX)
            with dve.Fori(0, NX) as j:
                with dve.If(j < more):
                    heads(j + NE)
                    tile(j + NE)
            last = more + NE
            for c in range(TC):
                add_scattered(c, ds(last, 1), at(c + 1, (last, 3)))
            dve.wait_ge(sem("y_added"), at(3, (last, 3)))
            dve.wait_ge(sem("gate_in"), 128)
            residual(dve, step, "moe", lambda c: yacc[:, c, :])

        @block.tensor
        def _(pe):
            pe.wait_ge(sem("ident_made"), 1)
            pe.wait_ge(sem("vec_in"), 16 * 14)
            pe.transpose(ps[:, 7, 0:80], vec[0:80, 0, :], ident[0:80, 0:80])
            pe.transpose(ps[:, 7, P:2 * P], vec[:, 1, :], ident[:, :])
            n = CW * DK - P
            pe.transpose(ps[:, 7, 2 * P:2 * P + n], vec[0:n, 2, :], ident[0:n, 0:n]).then_inc(sem("vec_turned"), 1)
            pe.wait_ge(sem("cst_made"), 1)

            def ada(layer, base):
                with pe.Fori(0, 4) as it:
                    for k in range(6):
                        if k % 2 == 0:
                            pe.wait_ge(sem(f"ada_row{layer}"), at(k // 2 + 1, (it, 3)))
                        s = base + k
                        pe.wait_ge(lo_made, at(s + 1, (it, 6)))
                        hi, lo = parts(s, 512, 4)
                        for i in range(4):
                            kk = 4 * (k % 2) + i
                            pe.matmul(ps[:, k // 2, :], cst[:, kk, :], hi[:, i, :], start=kk == 0, stop=False)
                            last = pe.matmul(ps[:, k // 2, :], cst[:, kk, :], lo[:, i, :], start=False, stop=kk == DK - 1)
                        last.then_inc(chunk_used, 1)
                pe.wait_ge(sem(f"ada_row{layer}"), 3 + 12)
                pe.wait_ge(sem(f"bias_in{layer}"), 16)
                for i in range(32):
                    m = (0, 1, 3, 4)[i // DK]
                    last = pe.transpose(ps[:, 3, 8 * i:8 * i + 5], mrow[0:5, m * D + (i % DK) * P:m * D + (i % DK + 1) * P],
                                        ident[0:5, 0:5])
                last.then_inc(sem(f"rows_turned{layer}"), 1)
                for i in range(4):
                    c0 = (2, 5)[i // 2] * D + i % 2 * 512
                    last = pe.matmul(ps[0:2, 4 + i, :], comb[:, :], mrow[0:5, c0:c0 + 512], start=True, stop=True)
                last.then_inc(sem(f"gate_rows{layer}"), 1)

            ada(0, 0)
            pe.wait_ge(sem("grow_made0"), 1)
            norm_pe(pe, "conv")
            for t in range(4):
                for i in range(2):
                    s = PW1 + 2 * t + i
                    pe.wait_ge(lo_made, s + 1)
                    hi, lo = parts(s, 256, DK)
                    for m in range(2):
                        if t >= 2:
                            pe.wait_ge(sem("glu_done"), 2 * (t - 1))
                        b = 4 * (t % 2) + 2 * i + m
                        for k in range(DK):
                            if t == 0 and i == 0 and m == 0:
                                pe.wait_ge(sem("conv_h_lo"), k + 1)
                            last = mm3(ps[:, b, 0:T], hi[:, k, m * P:(m + 1) * P], lo[:, k, m * P:(m + 1) * P],
                                       hTh[:, k, :], hTl[:, k, :], k == 0, k == DK - 1)
                    last.then_inc(chunk_used, 1)
            pe.wait_ge(sem("glu_done"), 8)
            ada(1, ADA1)
            pe.wait_ge(sem("ones_made"), 2)
            for j in range(DK):
                pe.wait_ge(sem("conv_done"), j + 1)
                last = pe.matmul(ps[:, 0, 0:CV], ones[:, :], v[:, j, :], start=j == 0, stop=j == DK - 1)
            last.then_inc(sem("ln_mean"), 1)
            for j in range(DK):
                pe.wait_ge(sem("ln_square"), j + 1)
                pe.matmul(ps[:, 1, 0:CV], ones[:, :], sq[:, j % 2, :], start=j == 0, stop=j == DK - 1)\
                    .then_inc(sem("ln_summed"), 1)

            def rows_product(s, q, h_lo, first, blocks):
                pe.wait_ge(lo_made, s + 1)
                hi, lo = parts(s, D, 2)
                for i in range(2):
                    k = 2 * q + i
                    pe.wait_ge(sem(h_lo), k + 1)
                    for c in range(TC):
                        for h in range(2):
                            last = mm3(ps[:, 2 * c + h, :], hTh[:, k, c * P:(c + 1) * P], hTl[:, k, c * P:(c + 1) * P],
                                       hi[:, i, h * 512:(h + 1) * 512], lo[:, i, h * 512:(h + 1) * 512],
                                       k == 0, k == blocks - 1)
                last.then_inc(chunk_used, 1)

            pe.wait_ge(sem("ln_root"), 1)
            for q in range(DK // 2):
                rows_product(PW2 + q, q, "ln_h_lo", q == 0, DK)

            norm_pe(pe, "ffn")

            def ffn_up(s, sub, silus, prods, ends, first=False, loop=None):
                for i, (bank, name, need) in enumerate(((6, "ffn_silu", silus), (7, "ffn_prod", prods))):
                    pe.wait_ge(lo_made, at(s + i + 1, loop))
                    if not first:
                        pe.wait_ge(sem(name), need)
                    hi, lo = parts(s + i, 256, DK)
                    if first:
                        pe.wait_ge(sem("ffn_modulated"), 2 * (DK - 1 + i))
                    for k in range(DK):
                        if first and i == 0:
                            pe.wait_ge(sem("ffn_h_lo"), k + 1)
                        last = mm3(ps[:, bank, 0:T], hi[:, k, sub * P:(sub + 1) * P], lo[:, k, sub * P:(sub + 1) * P],
                                   hTh[:, k, :], hTl[:, k, :], k == 0, k == DK - 1)
                    last.then_inc(ends, 1)

            def ffn_down(s, sub, made, ends, first=False, final=False, loop=None):
                pe.wait_ge(lo_made, at(s + 1, loop))
                pe.wait_ge(sem("ffn_lo"), made)
                hi, lo = parts(s, D, 2)
                for c in range(TC):
                    for h in range(2):
                        last = mm3(ps[:, 2 * c + h, :], fh[:, sub, c * P:(c + 1) * P], fl[:, sub, c * P:(c + 1) * P],
                                   hi[:, sub, h * 512:(h + 1) * 512], lo[:, sub, h * 512:(h + 1) * 512], first, final)
                last.then_inc(ends, 1)

            up, down = sem("ffn_up"), sem("ffn_down")
            pe.wait_ge(sem("conv_x"), TC)
            ffn_up(FFN, 0, 0, 0, up, first=True)
            ffn_up(FFN, 1, 1, 1, chunk_used)
            ffn_down(FFN + 2, 0, 1, down, first=True)
            ffn_up(FFN + 3, 0, 2, 2, up)
            ffn_down(FFN + 2, 1, 2, chunk_used)
            with pe.Fori(0, 4) as it:
                for i in (1, 2):
                    s = FFN + 3 * i
                    ffn_up(s, 1, at(2 * i + 1, (it, 4)), at(2 * i + 1, (it, 4)), chunk_used, loop=(it, 6))
                    ffn_down(s + 2, 0, at(2 * i + 1, (it, 4)), down, loop=(it, 6))
                    ffn_up(s + 3, 0, at(2 * i + 2, (it, 4)), at(2 * i + 2, (it, 4)), up, loop=(it, 6))
                    ffn_down(s + 2, 1, at(2 * i + 2, (it, 4)), chunk_used, loop=(it, 6))
            s = FFN + 27
            ffn_up(s, 1, 19, 19, chunk_used)
            ffn_down(s + 2, 0, 19, down)
            ffn_up(s + 3, 0, 20, 20, up)
            ffn_down(s + 2, 1, 20, chunk_used)
            ffn_up(s + 3, 1, 21, 21, chunk_used)
            ffn_down(s + 5, 0, 21, down)
            ffn_down(s + 5, 1, 22, chunk_used, final=True)

            norm_pe(pe, "mla")
            pe.wait_ge(sem("ffn_x"), TC)
            for n, width, b in ((0, QLR, 0), (2, KVR + RD, 3)):
                for i in range(2):
                    s = MLA + n + i
                    pe.wait_ge(lo_made, s + 1)
                    hi, lo = parts(s, width, 4)
                    for kk in range(4):
                        k = 4 * i + kk
                        pe.wait_ge(sem("mla_h_lo"), k + 1)
                        for c in range(TC):
                            last = mm3(ps[:, b + c, 0:width], hTh[:, k, c * P:(c + 1) * P], hTl[:, k, c * P:(c + 1) * P],
                                       hi[:, kk, :], lo[:, kk, :], k == 0, k == DK - 1)
                    last.then_inc(chunk_used, 1)
            pe.wait_ge(sem("cq_made"), TC)
            for k in range(4):
                if k >= 2:
                    pe.wait_ge(sem("cq_scaled"), k - 1)
                for c in range(TC):
                    last = pe.transpose(ps[:, 6 + k % 2, c * P:(c + 1) * P], xn[:, c, k * P:(k + 1) * P], ident[:, :])
                last.then_inc(sem("cq_turned"), 1)
            pe.wait_ge(sem("ckv_made"), TC)
            pe.wait_ge(sem("cache_in"), 32)
            for k in range(2):
                for c in range(KC):
                    last = pe.transpose(ps[:, k, c * P:(c + 1) * P], ckv[:, c, k * P:(k + 1) * P], ident[:, :])
                last.then_inc(sem("ck_turned"), 1)
            pe.wait_ge(sem("lat_split"), 4)

            with pe.Fori(0, NGRP) as g:
                for i in range(2):
                    kv, q = GRP + 2 * i, GRP + 2 * i + 1
                    n, pair = i + 1, (g, 2)
                    pe.wait_ge(lo_made, at(kv + 1, (g, 6)))
                    if i == 0:
                        pe.wait_ge(sem("att_y"), at(1, (g, 2)))
                    hi, lo = parts(kv, 512, 2)
                    for c in range(KC):
                        for k in range(2):
                            last = mm3(ps[:, c, :], ckTh[:, k, c * P:(c + 1) * P], ckTl[:, k, c * P:(c + 1) * P],
                                       hi[:, k, :], lo[:, k, :], k == 0, k == 1)
                    last.then_inc(chunk_used, 1)
                    pe.wait_ge(lo_made, at(q + 1, (g, 6)))
                    if i == 1:
                        pe.wait_ge(sem("oT_lo"), at(2, (g, 4)))
                    hi, lo = parts(q, 384, 4)
                    for c in range(TC):
                        for k in range(4):
                            last = mm3(ps[:, 4 + c, 0:384], cqTh[:, k, c * P:(c + 1) * P], cqTl[:, k, c * P:(c + 1) * P],
                                       hi[:, k, :], lo[:, k, :], k == 0, k == 3)
                    last.then_inc(chunk_used, 1)
                    pe.wait_ge(sem("k_scaled"), at(n, pair))
                    for h in range(2):
                        for c in range(KC):
                            pe.transpose(ps[:, h, c * P:(c + 1) * P], kv_sb[:, c, 256 * h:256 * h + P], ident[:, :])
                    for c in range(KC):
                        last = pe.transpose(ps[:, 2, c * P:(c + 1) * P], krh[:, c, :, :].rearrange("p a b -> p (a b)"), ident[:, :])
                    last.then_inc(sem("k_turned"), 1)
                    pe.wait_ge(sem("q_scaled"), at(n, pair))
                    for h in range(2):
                        for c in range(TC):
                            pe.transpose(ps[:, 3 + 4 * h, c * P:(c + 1) * P], q_sb[:, 2 * c + h, 0:P], ident[:, :])
                    for c in range(TC):
                        last = pe.transpose(ps[:, 4, c * P:(c + 1) * P],
                                            qr[:, 0, 2 * c:2 * c + 2, :].rearrange("p a b -> p (a b)"), ident[:, :])
                    last.then_inc(sem("q_turned"), 1)
                    pe.wait_ge(sem("kT_made"), at(3 * n, (g, 6)))
                    pe.wait_ge(sem("rT_made"), at(2 * n, (g, 4)))
                    for h in range(2):
                        r0, r1 = RD * h, RD * (h + 1)
                        for c in range(TC):
                            a, b = ((0, P), (P, 4 * P), (0, 3 * P))[c]
                            k0, k1 = (0, P) if c == 0 else (P, KC * P)
                            o = ps[:, 2 * h + c // 2, a:b]
                            pe.matmul(o, QB[:, h, c * P:(c + 1) * P], KT[:, h, k0:k1], start=True, stop=False)
                            last = pe.matmul(o, QB[r0:r1, 2, c * P:(c + 1) * P], KR[r0:r1, k0:k1], start=False, stop=True)
                        last.then_inc(sem("scored"), 1)
                    for h in range(2):
                        pe.wait_ge(sem("p_made"), at(6 * i + 3 * h + 3, (g, 12)))
                        for c in (1, 2):
                            for k in range(3):
                                o = P * (2 * k + c - 1)
                                pe.transpose(ps[:, 4 + o // 512, o % 512:o % 512 + P],
                                             pr[:, h, P + 3 * P * (c - 1) + k * P:2 * P + 3 * P * (c - 1) + k * P], ident[:, :])
                        pe.transpose(ps[:, 5, 2 * P:3 * P], pr[:, h, 0:P], ident[:, :]).then_inc(sem("p_turned"), 1)
                        pe.wait_ge(sem("pT_hi"), at(2 * i + h + 1, (g, 4)))
                        pe.wait_ge(sem("pT_lo"), at(2 * i + h + 1, (g, 4)))
                        v0 = 256 * h + P
                        pe.matmul(ps[:, 6 + h, 0:P], kv_sb[:, 0, v0:v0 + P], pT[:, 6 * P:7 * P], start=True, stop=True)
                        for k in range(3):
                            last = pe.matmul(ps[:, 6 + h, P:T], kv_sb[:, k + 1, v0:v0 + P], pT[:, 2 * P * k:2 * P * (k + 1)],
                                             start=k == 0, stop=k == 2)
                        last.then_inc(sem("o_made"), 1)
                pe.wait_ge(sem("oT_lo"), at(4, (g, 4)))
                for i in range(2):
                    s = GRP + 4 + i
                    pe.wait_ge(lo_made, at(s + 1, (g, 6)))
                    hi, lo = parts(s, 512, 4)
                    for c in range(TC):
                        for h in range(4):
                            last = mm3(ps[:, 3 * i + c, :], oTh[:, h, c * P:(c + 1) * P], oTl[:, h, c * P:(c + 1) * P],
                                       hi[:, h, :], lo[:, h, :], h == 0, h == 3)
                    last.then_inc(chunk_used, 1)

            norm_pe(pe, "moe")
            pe.wait_ge(sem("att_y"), 2 * NGRP + 1)
            for c in range(TC):
                for k in range(DK):
                    if c == 0:
                        pe.wait_ge(sem("moe_modulated"), 2 * k + 2)
                    last = pe.transpose(ps[:, 2 * c + k // 4, k % 4 * P:k % 4 * P + P], hf[:, k, c * P:(c + 1) * P], ident[:, :])
            last.then_inc(sem("tok_turned"), 1)
            pe.wait_ge(sem("router_in"), 16)
            for c in range(TC):
                for k in range(DK):
                    last = pe.matmul(ps[:, 6, c * NE:(c + 1) * NE], hf[:, k, c * P:(c + 1) * P], router[:, k, :],
                                     start=k == 0, stop=k == DK - 1)
            last.then_inc(sem("logits_made"), 1)
            pe.wait_ge(sem("gap_made"), 1)
            M = rt[:, 6, :, :]
            for c in range(TC):
                for b in range(c + 1):
                    pe.matmul(ps[:, 7, c * NE:(c + 1) * NE], before[:, :] if b == c else ones[:, :], M[:, b, :],
                              start=b == 0, stop=b == c)
            for b in range(TC):
                last = pe.matmul(ps[:, 7, TC * NE:(TC + 1) * NE], ones[:, :], M[:, b, :], start=b == 0, stop=b == TC - 1)
            last.then_inc(sem("ranked"), 1)
            pe.wait_ge(sem("tok_made"), TC)
            pe.wait_ge(sem("moe_const"), 7)
            pe.wait_ge(sem("tab_ready"), 1)

            def scatter():
                for c in range(TC):
                    for h in range(2):
                        o = ps[:, (0, 2, 6)[c] + h, :]
                        pe.matmul(o, selT[:, c * P:(c + 1) * P], yh[:, h * 512:(h + 1) * 512], start=True, stop=False)
                        last = pe.matmul(o, selT[:, c * P:(c + 1) * P], yl[:, h * 512:(h + 1) * 512], start=False, stop=True)
                    last.then_inc(sem("scattered"), 1)

            def tile(t):
                L = (t, TILE_CH)
                pe.wait_ge(sem("sel_made"), at(3, (t, 3)))
                for k in range(DK):
                    for c in range(TC):
                        last = pe.matmul(ps[:, 4 + k // 4, k % 4 * P:k % 4 * P + P], xn[:, c, k * P:(k + 1) * P], sel[:, c, :],
                                         start=c == 0, stop=c == TC - 1)
                last.then_inc(sem("gathered"), 1)
                pe.wait_ge(sem("y_lo"), at(1, (t, 1)))
                scatter()
                pe.wait_ge(sem("xg_lo"), at(1, (t, 1)))
                for c in range(TC):
                    last = pe.transpose(ps[:, 4, c * P:(c + 1) * P], sel[:, c, :], ident[:, :])
                last.then_inc(sem("sel_turned"), 1)

                def turn(g):
                    if g == 1:
                        pe.wait_ge(sem("selT_made"), at(1, (t, 1)))
                    pe.wait_ge(sem("hm_made"), at(g + 2, (t, 3)))
                    if g == 2:
                        pe.wait_ge(sem("hg_lo"), at(1, (t, 3)))
                    for i in range(4):
                        last = pe.transpose(ps[:, 5 - g % 2, i * P:(i + 1) * P], hm[:, g % 2, i * P:(i + 1) * P], ident[:, :])
                    last.then_inc(sem("hm_turned"), 1)

                for k in range(TILE_CH):
                    s = MOE + k
                    pe.wait_ge(lo_made, at(s + 1, L))
                    if k in (0, 4):
                        pe.wait_ge(sem("y_added"), at(k // 4 + 1, (t, 3)))
                    if k == 8:
                        pe.wait_ge(sem("hm_made"), at(2, (t, 3)))
                    if k == 12:
                        pe.wait_ge(sem("y_added"), at(3, (t, 3)))
                    if k >= 12 and k % 2 == 0:
                        pe.wait_ge(sem("hg_lo"), at((k - 12) // 2 + 1, (t, 3)))
                    if k < 12:
                        b = 2 * (k // 4 % 2) + k // 2 % 2
                        hi, lo = parts(s, 512, 4)
                        for i in range(4):
                            kk = 4 * (k % 2) + i
                            last = mm3(ps[:, b, :], xgh[:, kk, :], xgl[:, kk, :], hi[:, i, :], lo[:, i, :],
                                       kk == 0, kk == DK - 1)
                    else:
                        hi, lo = parts(s, D, 2)
                        for i in range(2):
                            f = 2 * (k - 12) + i
                            for h in range(2):
                                last = mm3(ps[:, 6 + h, :], hgh[:, f, :], hgl[:, f, :], hi[:, i, h * 512:(h + 1) * 512],
                                           lo[:, i, h * 512:(h + 1) * 512], f == 0, f == FE // P - 1)
                    last.then_inc(chunk_used, 1)
                    if k in (5, 9, 13):
                        turn(k // 4 - 1)

            with pe.Fori(0, NE) as e:
                tile(e)
            more = pe.value_load(tab[0:1, 0:1], min_val=0, max_val=NX)
            with pe.Fori(0, NX) as j:
                with pe.If(j < more):
                    tile(j + NE)
            pe.wait_ge(sem("y_lo"), at(1, (more + NE, 1)))
            scatter()


_OUTS = ["y_prompt", "y_sample", "new_ckv", "new_krope"]


def shape_tables(inputs):
    n = inputs["x_sample"].shape[1]
    rd = inputs["cache_krope"].shape[-1]
    ax = rd // 2
    pos = np.arange(n)
    inv = np.float32(ROPE_BASE) ** (-np.arange(0, ax, 2, dtype=np.float32) / np.float32(ax))
    ang = np.stack([(pos // GRID_W).astype(np.float32)[:, None] * inv, (pos % GRID_W).astype(np.float32)[:, None] * inv], 1)
    cos, sin = np.cos(ang), np.sin(ang)
    keys = inputs["x_prompt"].shape[1] + n + inputs["cache_ckv"].shape[2]
    tab = np.zeros((2, keys, rd), np.float32)
    tab[0] = 1.0
    p = inputs["x_prompt"].shape[1]
    tab[0, p:p + n] = np.stack([cos, cos], 2).reshape(n, rd)
    tab[1, p:p + n] = np.stack([-sin, sin], 2).reshape(n, rd)
    comb = np.zeros((5, 2), np.float32)
    for row, cond in ((0, 0), (2, 0), (4, 0), (1, 1), (3, 1), (4, 1)):
        comb[row, cond] = 1.0
    return {"rope_tab": tab, "comb_tab": comb}


def kernel(**inputs):
    import concourse.bacc as bacc
    from concourse.bass_utils import run_bass_kernel_spmd

    nc = bacc.Bacc("TRN2", target_bir_lowering=False, num_devices=1)
    given = {**inputs, **shape_tables(inputs)}
    arrays = {f"in_{n}": np.ascontiguousarray(a) for n, a in given.items()}
    d = {n: nc.dram_tensor(f"in_{n}", arrays[f"in_{n}"].shape, F32, kind="ExternalInput").ap() for n in given}
    (b, seq, dm), (db, dseq, _) = inputs["x_prompt"].shape, inputs["x_sample"].shape
    _, nm, _, rank = inputs["cache_ckv"].shape
    shapes = [(b, seq, dm), (db, dseq, dm), (b, nm, seq, rank), (b, nm, seq, inputs["cache_krope"].shape[-1])]
    out = {n: nc.dram_tensor(f"out_{n}", s, F32, kind="ExternalOutput").ap() for n, s in zip(_OUTS, shapes)}
    hybrid_conv_mla_diffusion_step(nc, d, out)
    r = run_bass_kernel_spmd(nc, [arrays], core_ids=[0])
    return tuple(r.results[0][f"out_{n}"] for n in _OUTS)
```

```python
import numpy as np
from contextlib import ExitStack

import concourse.bass as bass
from concourse import mybir

F32 = mybir.dt.float32
F32R = mybir.dt.float32r
I32 = mybir.dt.int32
ALU = mybir.AluOpType
ACT = mybir.ActivationFunctionType
AX = mybir.AxisListType.X
ds = bass.ds

P = 128
EPS = 1e-6
GRID_W = 64
ROPE_BASE = 10000.0
TOP_K = 2
CH = 2048
RAW = 6
HL = 3
BIG = 1000.0
GONE = -3.0e38
MAGIC = 0x5F3759DF


def at(v, loop=None, times=1):
    return v if loop is None else loop[0] * (loop[1] * times) + v


class Steps:

    def __init__(self, eng, sem):
        self.eng, self.sem, self.n, self.loop = eng, sem, 0, None

    def __call__(self, ins):
        ins.then_inc(self.sem, 1)
        self.n += 1
        self.eng.wait_ge(self.sem, at(self.n, self.loop))

    def begin(self, reg, per):
        self.loop, self.first, self.per = (reg, per), self.n, per

    def end(self, turns):
        assert self.n - self.first == self.per, (self.n - self.first, self.per)
        self.loop, self.n = None, self.first + self.per * turns


def hybrid_conv_mla_diffusion_step(nc, d, out):
    DEPTH, D, _ = d["ada_w"].shape
    DK = D // P
    NP_TOK = d["x_prompt"].shape[1]
    NS_TOK = d["x_sample"].shape[1]
    T = NP_TOK + NS_TOK
    TC = T // P
    PAST = d["cache_ckv"].shape[2]
    CW = d["conv_dw"].shape[1]
    PAD = CW // 2
    CU = PAD + NP_TOK + PAD + NS_TOK + PAD
    CV = CU - 2 * PAD
    SV = NP_TOK + PAD
    FF = d["ffn_w1"].shape[2]
    NF = FF // P
    QLR = d["mla_wdq"].shape[2]
    KVR = d["mla_kv_norm_g"].shape[1]
    QKD = d["mla_q_qk_g"].shape[1]
    RD = QKD - P
    NH = d["mla_wuq"].shape[2] // QKD
    NE = d["moe_router"].shape[2]
    FE = d["moe_w1"].shape[3]
    NG = FE // 512
    KC = (T + PAST) // P
    NX = (TOP_K * T - 1) // P
    NT = NE + NX + 1
    assert (DK, TC, KC, NP_TOK, QKD, KVR, QLR, NG) == (8, 3, 4, P, 192, 256, 512, 3)

    ADA_CH = 6 * D // 512 * 2
    PW1 = ADA_CH
    ADA1 = PW1 + 2 * D // 256
    PW2 = ADA1 + ADA_CH
    FFN = PW2 + DK // 2
    MLA = FFN + 3 * (NF // 2)
    GRP = MLA + 4
    NPAIR = NH // 2
    MOE = GRP + 3 * NPAIR
    TAPS, DVE_BLOCKS = 5, 5
    REST = DK - DVE_BLOCKS
    TURN_TAPS = (CW - 1) // 4
    FIRST_TAPS = CW - 4 * TURN_TAPS
    TILE_CH = 6 * NG
    MOEX = MOE + TILE_CH * NE

    ctx = ExitStack()
    with ctx:
        def sb(name, shape, dt=F32):
            return ctx.enter_context(nc.sbuf_tensor(name, shape, dt))

        def share(name, *groups):
            made, most = [], 0
            for group in groups:
                with ExitStack() as s:
                    made.append([s.enter_context(nc.sbuf_tensor(n, shape, dt)) for n, shape, dt in group])
                most = max(most, sum(-(-int(np.prod(shape[1:])) * 4 // 64) * 16 for _, shape, _ in group))
            sb(name, [P, most])
            return made

        raw = sb("raw", [P, RAW, CH])
        wh = sb("wh", [P, HL, CH], F32R)
        wl = sb("wl", [P, HL, CH], F32R)
        x = sb("x", [P, TC, D])
        ident = sb("ident", [P, P])
        ones = sb("ones", [P, P])
        vT = sb("vT", [P, 64])
        modv = sb("modv", [P, DEPTH, 2, 4, DK])
        modA = sb("modA", [P, DEPTH, 2, 2, DK])
        st = sb("st", [P, 64])
        nr = sb("nr", [P, 3, 16])
        nri = sb("nri", [P, 2, 16], I32)
        comb = sb("comb", [3, 2])
        epsc = sb("epsc", [P, 1])

        gate = sb("gate", [P, 2, D])
        (mrow,), (hTh, hTl), (cqTh, cqTl, ckTh, ckTl, kr_rot, tq), (xgh, xgl, hm, hgh, hgl) = share(
            "shared24",
            [("mrow", [P, 6 * D], F32)],
            [("hTh", [P, DK, T], F32R), ("hTl", [P, DK, T], F32R)],
            [("cqTh", [P, 4, T], F32R), ("cqTl", [P, 4, T], F32R), ("ckTh", [P, 2, KC * P], F32R),
             ("ckTl", [P, 2, KC * P], F32R), ("kr_rot", [P, KC, RD], F32), ("tq", [P, 2, 2 * TC, RD], F32)],
            [("xgh", [P, DK, P], F32R), ("xgl", [P, DK, P], F32R), ("hm", [P, 2, 512], F32),
             ("hgh", [P, FE // P, P], F32R), ("hgl", [P, FE // P, P], F32R)])
        (xn,), (v,), (k_sb, v_sb) = share(
            "shared12a",
            [("xn", [P, TC, D], F32)],
            [("v", [P, DK, CV], F32)],
            [("k_sb", [P, KC, 2, P], F32), ("v_sb", [P, 2, KC, 2, P], F32)])
        (hf,), (yacc,), (cqf, ckv) = share(
            "shared12b",
            [("hf", [P, DK, T], F32)],
            [("yacc", [P, TC, D], F32)],
            [("cqf", [P, 4, T], F32), ("ckv", [P, KC, KVR + RD], F32)])
        ((vec, cnd, cst, mT, grow, dwT, u, sig), (_, _, _, _, _, _, _, sq, sd, rs), (fs, ff, fh, fl),
         (q_sb, qr, KT, QB, pT, oTh, oTl, krh, KR, pr),
         (yh, yl, sel, selT, ms, R, G, rt, jt, tab, xj, xw, js, upto, lgT, before, iota, router)) = share(
            "own",
            [("vec", [P, 3, P], F32), ("cnd", [2 * DK, P], F32), ("cst", [P, DK, 2], F32), ("mT", [P, 32, 3], F32), ("grow", [2, 4, 512], F32),
             ("dwT", [P, CW * DK], F32), ("u", [P, DK, CU], F32), ("sig", [P, 2, 2, T], F32)],
            [("vec_", [P, 3, P], F32), ("cnd_", [2 * DK, P], F32), ("cst_", [P, DK, 2], F32), ("mT_", [P, 32, 3], F32),
             ("grow_", [2, 4, 512], F32), ("dwT_", [P, CW * DK], F32), ("u_", [P, DK, CU], F32),
             ("sq", [P, 2, CV], F32), ("sd", [P, CV], F32), ("rs", [P, CV], F32)],
            [("fs", [P, 2, T], F32), ("ff", [P, 2, T], F32), ("fh", [P, 2, T], F32R), ("fl", [P, 2, T], F32R)],
            [("q_sb", [P, 2 * TC, QKD], F32), ("qr", [P, 2, 2 * TC, RD], F32), ("KT", [P, 2, KC * P], F32),
             ("QB", [P, 3, T], F32), ("pT", [P, 2, 7 * P], F32), ("oTh", [P, 2, T], F32R), ("oTl", [P, 2, T], F32R),
             ("krh", [P, KC, 2, RD], F32), ("KR", [P, KC * P], F32), ("pr", [P, 2, 7 * P], F32)],
            [("yh", [P, D], F32R), ("yl", [P, D], F32R), ("sel", [P, TC, P], F32), ("selT", [P, T], F32R),
             ("ms", [P, 512], F32), ("R", [P, TC, NT], F32), ("G", [P, TC, NT + 1], F32),
             ("rt", [P, 12, TC, NE], F32), ("jt", [P, 12, NE], F32), ("tab", [1, 16], I32),
             ("xj", [P, 3, NX, NE], F32), ("xw", [P, TC, NX, NE], F32), ("js", [P, NX, NE], F32), ("upto", [P, NE, NE], F32), ("lgT", [NE, T], F32),
             ("before", [P, P], F32), ("iota", [P, P], F32), ("router", [P, DK, NE], F32)])
        ps = ctx.enter_context(nc.psum_tensor("ps", [P, 8, 512], F32))
        gates_dram = nc.dram_tensor("gates_dram", [DEPTH, 2, 2, D], F32, kind="Internal").ap()

        tk = pT[:, 1, 0:2 * KC * RD].rearrange("p (i c r) -> p i c r", i=2, c=KC)
        gb = pT[:, 0, 2 * P:2 * P + 2 * RD + KVR]

        tap = sig[:, :, :, :].rearrange("p a b t -> p (a b t)").rearrange("p (i t) -> p i t", i=3)

        N1G, N2G, DWB, LNG, LNB, QNG, QKG, KKG = 0, 16, 32, 40, 48, 56, 62, 63
        VROWS = [("norm1_g", None), ("norm2_g", None), ("conv_dw_b", None), ("conv_ln_g", None), ("conv_ln_b", None),
                 ("mla_q_norm_g", None), ("mla_kv_norm_g", None)]

        named = {}

        def sem(name):
            if name not in named:
                named[name] = ctx.enter_context(nc.semaphore(name))
            return named[name]

        raw_in = [sem(f"raw_in{i}") for i in range(RAW)]
        hi_made, lo_made = sem("hi_made"), sem("lo_made")
        chunk_used = sem("chunk_used")

        def whole(s):
            return s < PW1 or ADA1 <= s < PW2

        def split_no(s):
            return s - ADA_CH if s < ADA1 else s - 2 * ADA_CH

        def load(sp, s, src, view, loop=None):
            if s >= RAW and whole(s - RAW):
                sp.wait_ge(chunk_used, at(s - RAW + 1, loop))
            elif s >= RAW:
                sp.wait_ge(hi_made, at(split_no(s - RAW) + 1, loop))
                sp.wait_ge(lo_made, at(split_no(s - RAW) + 1, loop))
            sp.dma_start(view(raw[:, s % RAW, :]), src).then_inc(raw_in[s % RAW], 16)

        def free_parts(eng, s, loop):
            if split_no(s) >= HL:
                before_it = s - HL if s < ADA1 or s >= PW2 + HL else s - HL - ADA_CH
                eng.wait_ge(chunk_used, at(before_it + 1, loop))

        def wait_parts(pe, s, loop=None):
            pe.wait_ge(lo_made, at(split_no(s) + 1, loop))

        def make_hi(act, s, loop=None):
            turns = None if loop is None else (loop[0], loop[1] // RAW * 16)
            act.wait_ge(raw_in[s % RAW], at(16 * (s // RAW + 1), turns))
            free_parts(act, s, loop)
            act.activation(wh[:, s % HL, :], raw[:, s % RAW, :], ACT.Copy).then_inc(hi_made, 1)

        def make_lo(eng, s, loop=None):
            eng.wait_ge(hi_made, at(split_no(s) + 1, loop))
            free_parts(eng, s, loop)
            eng.tensor_tensor(wl[:, s % HL, :], raw[:, s % RAW, :], wh[:, s % HL, :],
                              ALU.subtract).then_inc(lo_made, 1)

        def parts(s, n, k):
            return [t[:, s % HL, 0:k * n].rearrange("p (k n) -> p k n", k=k) for t in (wh, wl)]

        def rows(w, k0, k, c0, n):
            return w.rearrange("(k p) n -> p k n", p=P)[:, k0:k0 + k, c0:c0 + n]

        def as_rows(n, k):
            return lambda slot: slot[:, 0:k * n].rearrange("p (k n) -> p k n", k=k)

        def mm3(out_, sh, sl, mh, ml, start, stop):
            nc.tensor.matmul(out_, sh, mh, start=start, stop=False)
            nc.tensor.matmul(out_, sh, ml, start=False, stop=False)
            return nc.tensor.matmul(out_, sl, mh, start=False, stop=stop)

        def rsqrt(step, dst, src, n, shape=None):
            a, b, y = nr[:, 0, 0:n], nr[:, 1, 0:n], nr[:, 2, 0:n]
            dve = nc.vector
            step(dve.tensor_scalar(a, src, EPS, None, ALU.add))
            step(dve.tensor_scalar(nri[:, 0, 0:n], a.bitcast(I32), 1, None, ALU.logical_shift_right))
            step(dve.tensor_scalar(y.bitcast(I32), nri[:, 0, 0:n], -1, MAGIC, ALU.mult, ALU.add))
            for i in range(3):
                step(dve.tensor_tensor(b, y, y, ALU.mult))
                step(dve.scalar_tensor_tensor(out=b, in0=b, scalar=-0.5, in1=a, op0=ALU.mult, op1=ALU.mult))
                step(dve.scalar_tensor_tensor(out=y if i < 2 else dst, in0=b, scalar=1.5, in1=y,
                                              op0=ALU.add, op1=ALU.mult))

        RSQRT_STEPS = 12

        def norm_act(act, q, layer, n, before_, count):
            for c in range(TC):
                act.wait_ge(sem(before_), max(count, c + 1))
                act.activation(xn[:, c, :], x[:, c, :], ACT.Square, scale=D ** -0.5,
                               accum_out=st[:, c:c + 1]).then_inc(sem(q + "_squares"), 1)
            act.wait_ge(sem(q + "_rstd"), 1)
            act.activation(xn[:, 1, :], x[:, 1, :], ACT.Copy, scale=st[:, 5:6]).then_inc(sem(q + "_normed"), 1)
            act.wait_ge(sem(f"mod_ready{layer}"), 1)
            for j in range(DK):
                act.wait_ge(sem(q + "_turned"), j + 1)
                for cond, a, b in ((1, 0, P), (0, P, T)):
                    act.activation(hf[:, j, a:b], ps[:, 6 + j % 2, a:b], ACT.Identity,
                                   scale=modA[:, layer, n, cond, j:j + 1],
                                   bias=modv[:, layer, cond, 2 * n, j:j + 1]).then_inc(sem(q + "_modulated"), 1)

        def norm_dve(dve, step, q):
            dve.wait_ge(sem(q + "_squares"), TC)
            rsqrt(step, st[:, 4:4 + TC], st[:, 0:TC], TC)
            dve.sem_inc(sem(q + "_rstd"), 1)
            for c in (0, 2):
                dve.tensor_scalar(xn[:, c, :], x[:, c, :], st[:, 4 + c:5 + c], None,
                                  ALU.mult).then_inc(sem(q + "_normed"), 1)

        def norm_pe(pe, q):
            pe.wait_ge(sem(q + "_normed"), TC)
            for j in range(DK):
                if j >= 2:
                    pe.wait_ge(sem(q + "_modulated"), 2 * (j - 1))
                for c in range(TC):
                    last = pe.transpose(ps[:, 6 + j % 2, c * P:(c + 1) * P], xn[:, c, j * P:(j + 1) * P], ident[:, :])
                last.then_inc(sem(q + "_turned"), 1)

        def split_dve(dve, q, made, per):
            for j in range(DK):
                dve.wait_ge(sem(made), per * (j + 1))
                dve.tensor_copy(hTh[:, j, :], hf[:, j, :]).then_inc(sem(q + "_h_hi"), 1)
                dve.wait_ge(sem(q + "_h_hi"), j + 1)
                dve.tensor_tensor(hTl[:, j, :], hf[:, j, :], hTh[:, j, :], ALU.subtract).then_inc(sem(q + "_h_lo"), 1)

        def residual(dve, step, q, y):
            for c in range(TC):
                step(dve.tensor_tensor(xn[:, c, :], y(c), gate[:, 1 if c == 0 else 0, :], ALU.mult))
                dve.tensor_tensor(x[:, c, :], x[:, c, :], xn[:, c, :], ALU.add).then_inc(sem(q + "_x"), 1)
            dve.wait_ge(sem(q + "_x"), TC)

        def kv_chunk(n):
            return GRP if n == 0 else GRP + 3 * n - 1

        def turns(g=None):
            return lambda r: None if g is None else (g, 2 * r)

        block = ctx.enter_context(nc.Block())

        @block.sync
        def _(sp):
            sp.wait_ge(sem("cond_in"), 32)
            for layer, base in ((0, 0), (1, ADA1)):
                if layer == 1:
                    for t in range(4):
                        for i in range(2):
                            load(sp, PW1 + 2 * t + i, rows(d["conv_pw1"][0], 0, DK, i * D + t * 256, 256), as_rows(256, DK))
                w = d["ada_w"][layer].rearrange("(k p) n -> p k n", p=P)
                for k in range(6):
                    load(sp, base + k, w[:, 4 * (k % 2):4 * (k % 2) + 4, 512 * (k // 2):512 * (k // 2) + 512], as_rows(512, 4))
                with sp.Fori(1, 4) as it:
                    for k in range(6):
                        sp.wait_ge(chunk_used, at(base + k + 1 - RAW, (it, 6)))
                        slot = (base + k) % RAW
                        sp.dma_start(as_rows(512, 4)(raw[:, slot, :]), w[:, 4 * (k % 2):4 * (k % 2) + 4, ds(it * 1536 + 512 * (k // 2), 512)])\
                            .then_inc(raw_in[slot], 16)
            for q in range(DK // 2):
                load(sp, PW2 + q, rows(d["conv_pw2"][0], 2 * q, 2, 0, D), as_rows(D, 2))
            w1, w3 = (d[n][0].rearrange("(k p) n -> p k n", p=P) for n in ("ffn_w1", "ffn_w3"))
            w2 = d["ffn_w2"][0].rearrange("(k p) n -> p k n", p=P)
            sp.wait_ge(chunk_used, PW2)
            with sp.Fori(0, 5) as it:
                for i in range(2):
                    s = FFN + 3 * i
                    load(sp, s, w1[:, :, ds(it * 512 + 256 * i, 256)], as_rows(256, DK), (it, 6))
                    load(sp, s + 1, w3[:, :, ds(it * 512 + 256 * i, 256)], as_rows(256, DK), (it, 6))
                    load(sp, s + 2, w2[:, ds(it * 4 + 2 * i, 2), :], as_rows(D, 2), (it, 6))
            s = FFN + 30
            load(sp, s, w1[:, :, FF - 256:FF], as_rows(256, DK))
            load(sp, s + 1, w3[:, :, FF - 256:FF], as_rows(256, DK))
            load(sp, s + 2, w2[:, NF - 2:NF, :], as_rows(D, 2))
            for i in range(2):
                load(sp, MLA + i, rows(d["mla_wdq"][0], 4 * i, 4, 0, QLR), as_rows(QLR, 4))
            for i in range(2):
                load(sp, MLA + 2 + i, rows(d["mla_wdkv"][0], 4 * i, 4, 0, KVR + RD), as_rows(KVR + RD, 4))
            wuq, wukv, wo = (d[n][0].rearrange("(k p) n -> p k n", p=P) for n in ("mla_wuq", "mla_wukv", "mla_wo"))
            def load_proj(s, pair, loop=None):
                load(sp, s, wukv[:, :, ds(pair * 512, 512)], as_rows(512, 2), loop)
                load(sp, s + 1, wuq[:, :, ds(pair * 384, 384)], as_rows(384, 4), loop)

            def load_out(s, pair, loop=None):
                load(sp, s, wo[:, ds(pair * 2, 2), :], as_rows(D, 2), loop)

            load_proj(GRP, 0)
            with sp.Fori(0, NPAIR // 2 - 1) as g:
                for i in range(2):
                    load_proj(GRP + 3 * i + 2, g * 2 + i + 1, (g, 6))
                    load_out(GRP + 3 * i + 4, g * 2 + i, (g, 6))
            load_proj(MOE - 4, NPAIR - 1)
            load_out(MOE - 2, NPAIR - 2)
            load_out(MOE - 1, NPAIR - 1)

            ew1, ew3 = (d[n][0].rearrange("e (k p) n -> p e k n", p=P) for n in ("moe_w1", "moe_w3"))
            ew2 = d["moe_w2"][0].rearrange("e (k p) n -> p e k n", p=P)

            def load_tile(t, e):
                for g in range(NG):
                    for i in range(4):
                        w = (ew1, ew3)[i // 2]
                        load(sp, MOE + 4 * g + i, w[:, e, 4 * (i % 2):4 * (i % 2) + 4, 512 * g:512 * g + 512],
                             as_rows(512, 4), (t, TILE_CH))
                for i in range(6):
                    load(sp, MOE + 4 * NG + i, ew2[:, e, 2 * i:2 * i + 2, :], as_rows(D, 2), (t, TILE_CH))

            with sp.Fori(0, NE) as e:
                load_tile(e, e)
            sp.wait_ge(sem("tab_ready"), 1)
            more = sp.value_load(tab[0:1, 0:1], min_val=0, max_val=NX)
            with sp.Fori(0, NX) as j:
                with sp.If(j < more):
                    load_tile(j + NE, sp.value_load(tab[0:1, ds(j + 1, 1)], min_val=0, max_val=NE - 1))
            for c in range(TC):
                sp.wait_ge(sem("moe_x"), c + 1)
                dst = out["y_prompt"][0] if c == 0 else out["y_sample"][0, (c - 1) * P:c * P, :]
                sp.dma_start(dst, x[:, c, :]).then_inc(sem("y_out"), 16)
            sp.wait_ge(sem("y_out"), 16 * TC)
            sp.wait_ge(sem("kv_out"), 32)

        @block.gpsimd
        def _(pool):
            pool.memset(ident[:, :], 0.0).then_inc(sem("pool_steps"), 1)
            pool.memset(ones[:, :], 1.0).then_inc(sem("ones_made"), 1)
            pool.memset(epsc[:, :], EPS).then_inc(sem("ones_made"), 1)
            pool.wait_ge(sem("pool_steps"), 1)
            pool.affine_select(out=ident[:, :], in_=ident[:, :], compare_op=ALU.not_equal, fill=1.0, base=0,
                               pattern=[[-1, P]], channel_multiplier=1).then_inc(sem("ident_made"), 1)
            pool.memset(u[:, :, :], 0.0).then_inc(sem("u_zero"), 1)

            def fetch_gate(layer, which):
                for cond in range(2):
                    pool.dma_start(gate[:, cond, :], gates_dram[layer, cond, which].partition_broadcast(P))\
                        .then_inc(sem("gate_in"), 16)

            pool.wait_ge(sem("gates_out0"), 16)
            fetch_gate(0, 0)
            pool.wait_ge(chunk_used, ADA1)
            pool.dma_start(mrow[2:3, :], d["ada_b"][1:2, :]).then_inc(sem("bias_in1"), 16)
            def add_tap(w, loop=None):
                for i in range(REST):
                    pool.wait_ge(sem("tap_made"), at(REST * w + i + 1, loop))
                    if w > 1:
                        pool.wait_ge(sem("pool_taps"), at(REST * (w - 2) + i + 1, loop))
                    pool.tensor_tensor(v[:, DVE_BLOCKS + i, :], v[:, DVE_BLOCKS + i, :], tap[:, i, 0:CV],
                                       ALU.add).then_inc(sem("pool_taps"), 1)

            for w in range(1, FIRST_TAPS):
                add_tap(w)
            with pool.Fori(0, 4) as it:
                for w in range(FIRST_TAPS, FIRST_TAPS + TURN_TAPS):
                    add_tap(w, (it, REST * TURN_TAPS))
            pool.wait_ge(sem("conv_x"), TC)
            fetch_gate(0, 1)
            pool.wait_ge(sem("ffn_x"), TC)
            for i in range(2):
                pool.dma_start(tk[:, i, :, :], d["rope_tab"][i].rearrange("(c p) r -> p c r", p=P)).then_inc(sem("tk_in"), 16)
            pool.dma_start(gb[:, 0:RD], d["mla_q_qk_g"][0, P:QKD].partition_broadcast(P)).then_inc(sem("tk_in"), 16)
            pool.dma_start(gb[:, RD:2 * RD], d["mla_k_qk_g"][0, P:QKD].partition_broadcast(P)).then_inc(sem("tk_in"), 16)
            pool.dma_start(gb[:, 2 * RD:2 * RD + KVR], d["mla_kv_norm_g"][0].partition_broadcast(P)).then_inc(sem("tk_in"), 16)
            pool.wait_ge(sem("mla_h_lo"), DK)
            pool.dma_start(ckv[:, KC - 1, 0:KVR], d["cache_ckv"][0, 0]).then_inc(sem("cache_in"), 16)
            pool.dma_start(ckv[:, KC - 1, KVR:KVR + RD], d["cache_krope"][0, 0]).then_inc(sem("cache_in"), 16)
            pool.wait_ge(lo_made, split_no(GRP))
            make_lo(pool, GRP)
            make_lo(pool, GRP + 1)
            pool.wait_ge(chunk_used, MLA + 4)
            for i in range(2):
                for h in range(2):
                    dst = tq[:, i, :, :].rearrange("p (c h) r -> p c h r", h=2)[:, :, h, :]
                    pool.dma_start(dst, d["rope_tab"][i, 0:T, :].rearrange("(c p) r -> p c r", p=P)).then_inc(sem("tq_in"), 16)
            make_lo(pool, GRP + 2)
            pool.wait_ge(sem("ckv_made"), TC)
            pool.dma_start(out["new_ckv"][0, 0], ckv[:, 0, 0:KVR]).then_inc(sem("kv_out"), 16)
            pool.dma_start(out["new_krope"][0, 0], ckv[:, 0, KVR:KVR + RD]).then_inc(sem("kv_out"), 16)
            pool.wait_ge(sem("kv_out"), 32)
            pool.wait_ge(sem("lat_split"), 4)
            pool.wait_ge(sem("kr_ready"), 1)
            pool.memset(yacc[:, :, :], 0.0).then_inc(sem("yacc_zero"), 1)
            pool.wait_ge(sem("gates_out1"), 16)
            fetch_gate(1, 0)
            pool.wait_ge(sem("att_y"), TC * NPAIR + 1)
            pool.dma_start(router[:, :, :], d["moe_router"][0].rearrange("(k p) e -> p k e", p=P)).then_inc(sem("router_in"), 16)
            pool.memset(before[:, :], 1.0).then_inc(sem("moe_const"), 1)
            pool.iota(iota[:, :], pattern=[[1, P]], base=0, channel_multiplier=0,
                      allow_small_or_imprecise_dtypes=True).then_inc(sem("moe_const"), 1)
            pool.iota(js[:, :, :], pattern=[[1, NX], [0, NE]], base=0, channel_multiplier=0,
                      allow_small_or_imprecise_dtypes=True).then_inc(sem("moe_const"), 1)
            pool.memset(upto[:, :, :], 1.0).then_inc(sem("moe_const"), 1)
            pool.memset(G[:, :, 0:1], 0.0).then_inc(sem("moe_const"), 1)
            pool.memset(yh[:, :].bitcast(F32), 0.0).then_inc(sem("moe_const"), 1)
            pool.memset(yl[:, :].bitcast(F32), 0.0).then_inc(sem("moe_const"), 1)
            pool.memset(selT[:, :].bitcast(F32), 0.0).then_inc(sem("moe_const"), 1)
            pool.wait_ge(sem("moe_const"), 8)
            pool.affine_select(out=upto[:, :, :], in_=upto[:, :, :], compare_op=ALU.is_ge, fill=0.0, base=0,
                               pattern=[[1, NE], [-1, NE]], channel_multiplier=0).then_inc(sem("moe_const"), 1)
            pool.affine_select(out=before[:, :], in_=before[:, :], compare_op=ALU.is_gt, fill=0.0, base=0,
                               pattern=[[1, P]], channel_multiplier=-1).then_inc(sem("moe_const"), 1)
            pool.wait_ge(sem("mla_x"), TC)
            fetch_gate(1, 1)
            pool.wait_ge(sem("tok_turned"), 1)
            pool.memset(yacc[:, :, :], 0.0).then_inc(sem("yacc_zero"), 1)
            pool.wait_ge(sem("gate_in"), 8 * 16)

        @block.scalar
        def _(act):
            for i, c in enumerate((d["c"][0], d["c_ctx"])):
                act.dma_start(cnd[DK * i:DK * (i + 1), :], c.rearrange("(k p) -> k p", p=P)).then_inc(sem("cond_in"), 16)

            def vrow(n, src):
                k = src.shape[0]
                act.dma_start(vec[n:n + k, 0, :], src).then_inc(sem("vec_in"), 16)
            for n, name in ((N1G, "norm1_g"), (N2G, "norm2_g"), (DWB, "conv_dw_b"), (LNG, "conv_ln_g"), (LNB, "conv_ln_b"),
                            (QNG, "mla_q_norm_g"), (QNG + 4, "mla_kv_norm_g")):
                vrow(n, d[name].rearrange("a (k p) -> (a k) p", p=P))
            vrow(QKG, d["mla_q_qk_g"][0:1, 0:P])
            vrow(KKG, d["mla_k_qk_g"][0:1, 0:P])
            taps = d["conv_dw"][0].rearrange("w (k p) -> (w k) p", p=P)
            act.dma_start(vec[:, 1, :], taps[0:P, :]).then_inc(sem("vec_in"), 16)
            act.dma_start(vec[0:CW * DK - P, 2, :], taps[P:CW * DK, :]).then_inc(sem("vec_in"), 16)
            act.dma_start(comb[:, :], d["comb_tab"]).then_inc(sem("vec_in"), 16)
            act.dma_start(x[:, 0, :], d["x_prompt"][0]).then_inc(sem("x_in"), 16)
            act.dma_start(x[:, 1:3, :], d["x_sample"][0].rearrange("(c p) n -> p c n", p=P)).then_inc(sem("x_in"), 16)
            act.dma_start(mrow[2:3, :], d["ada_b"][0:1, :]).then_inc(sem("bias_in0"), 16)

            def tap_product(w, i, first=0, loop=None):
                j = DVE_BLOCKS + i
                if w == 0:
                    act.activation(v[:, j, :], u[:, j, 0:CV], ACT.Identity, scale=dwT[:, j:j + 1],
                                   bias=vT[:, DWB + j:DWB + j + 1]).then_inc(sem("tap_made"), 1)
                    return
                if w > 1:
                    act.wait_ge(sem("pool_taps"), at(REST * (w - 2) + i + 1, loop))
                act.activation(tap[:, i, 0:CV], u[:, j, ds(first + w, CV)], ACT.Copy,
                               scale=dwT[:, ds(first * DK + w * DK + j, 1)]).then_inc(sem("tap_made"), 1)

            def ada_rows(layer, base):
                n = REST * TURN_TAPS // 3
                act.sem_inc(sem(f"ada_row{layer}"), 3)
                with act.Fori(0, 4) as it:
                    for b in range(3):
                        if layer:
                            for m in range(b * n, (b + 1) * n):
                                tap_product(FIRST_TAPS + m // REST, m % REST, it * TURN_TAPS, (it, REST * TURN_TAPS))
                        act.wait_ge(chunk_used, at(base + 2 * b + 2, (it, 6)))
                        act.activation(mrow[0:2, ds(it * 1536 + 512 * b, 512)], ps[0:2, b, :],
                                       ACT.Copy).then_inc(sem(f"ada_row{layer}"), 1)

            def ada_gates(layer):
                act.wait_ge(sem(f"gate_rows{layer}"), 1)
                if layer:
                    act.wait_ge(sem("gates_out0"), 16)
                act.activation(grow[:, :, :], ps[0:2, 4:8, :], ACT.Copy).then_inc(sem(f"grow_made{layer}"), 1)
                act.wait_ge(sem(f"grow_made{layer}"), 1)
                act.dma_start(gates_dram[layer].rearrange("c w n -> c (w n)"), grow[:, :, :].rearrange("c k n -> c (k n)"))\
                    .then_inc(sem(f"gates_out{layer}"), 16)

            act.wait_ge(sem("cond_turned"), 1)
            act.activation(cst[:, :, :], ps[:, 7, 0:2 * DK].rearrange("p (s k) -> p k s", k=DK), ACT.Silu).then_inc(sem("cst_made"), 1)
            ada_rows(0, 0)
            ada_gates(0)
            for s in range(3):
                make_hi(act, PW1 + s)
            norm_act(act, "conv", 0, 0, "x_in", 32)
            for t in range(4):
                if t < 3:
                    make_hi(act, PW1 + 2 * t + 3)
                act.wait_ge(chunk_used, PW1 + 2 * t + 2)
                if t >= 2:
                    act.wait_ge(sem("glu_done"), 2 * (t - 1))
                b = 4 * (t % 2) + 2
                act.activation(sig[:, t % 2, :, :], ps[:, b:b + 2, 0:T], ACT.Sigmoid).then_inc(sem("sig_made"), 1)
                if t < 2:
                    make_hi(act, PW1 + 2 * t + 4)
            act.wait_ge(sem("glu_done"), 8)
            act.wait_ge(sem("dw_made"), 2)
            for w in range(FIRST_TAPS):
                for i in range(REST):
                    tap_product(w, i)
            ada_rows(1, ADA1)
            for q in range(3):
                make_hi(act, PW2 + q)
            ada_gates(1)
            for j in range(DK):
                act.wait_ge(sem("ln_centred"), j + 1)
                if j >= 2:
                    act.wait_ge(sem("ln_summed"), j - 1)
                act.activation(sq[:, j % 2, :], v[:, j, :], ACT.Square).then_inc(sem("ln_square"), 1)
            act.wait_ge(sem("ln_summed"), DK)
            act.activation(sd[:, :], ps[:, 1, 0:CV], ACT.Sqrt, scale=1.0 / D, bias=epsc[:, 0:1]).then_inc(sem("ln_root"), 1)
            for j in range(DK):
                act.wait_ge(sem("ln_scaled"), j + 1)
                for a, b, o in ((0, P, 0), (P, T, SV - P)):
                    act.activation(hf[:, j, a:b], v[:, j, a + o:b + o], ACT.Silu, scale=vT[:, LNG + j:LNG + j + 1],
                                   bias=vT[:, LNB + j:LNB + j + 1]).then_inc(sem("ln_done"), 1)
            for q in range(DK // 2):
                make_hi(act, PW2 + q + 3)
            norm_act(act, "ffn", 0, 1, "conv_x", 0)
            act.wait_ge(sem("gates_out1"), 16)

            def gate_silu(b, value, loop, free=True):
                if free:
                    act.wait_ge(sem("ffn_prod"), at(value - 2, loop))
                act.activation(fs[:, b, :], ps[:, 6, 0:T], ACT.Silu).then_inc(sem("ffn_silu"), 1)

            act.wait_ge(sem("ffn_up"), 1)
            gate_silu(0, 1, None, False)
            act.wait_ge(chunk_used, FFN + 1)
            gate_silu(1, 2, None, False)
            make_hi(act, FFN + 3)
            make_hi(act, FFN + 4)
            act.wait_ge(sem("ffn_up"), 3)
            gate_silu(0, 3, None)
            make_hi(act, FFN + 5)
            with act.Fori(0, 4) as it:
                for i in (1, 2):
                    act.wait_ge(chunk_used, at(FFN + 3 * i + 1, (it, 6)))
                    gate_silu(1, 2 * i + 2, (it, 4))
                    make_hi(act, FFN + 3 * i + 3, (it, 6))
                    make_hi(act, FFN + 3 * i + 4, (it, 6))
                    act.wait_ge(sem("ffn_up"), at(2 * i + 3, (it, 4)))
                    gate_silu(0, 2 * i + 3, (it, 4))
                    make_hi(act, FFN + 3 * i + 5, (it, 6))
            act.wait_ge(chunk_used, FFN + 28)
            gate_silu(1, 20, None)
            make_hi(act, FFN + 30)
            make_hi(act, FFN + 31)
            act.wait_ge(sem("ffn_up"), 21)
            gate_silu(0, 21, None)
            make_hi(act, FFN + 32)
            act.wait_ge(chunk_used, FFN + 31)
            gate_silu(1, 22, None)
            for i in range(3):
                make_hi(act, MLA + i)
            norm_act(act, "mla", 1, 0, "ffn_x", 0)
            make_hi(act, MLA + 3)
            act.wait_ge(chunk_used, MLA + 2)
            for c in range(TC):
                act.activation(q_sb[:, 0:3, 0:QKD].rearrange("p a b -> p (a b)")[:, 0:QLR] if c == 0 else KT[:, c - 1, :],
                               ps[:, c, :], ACT.Square, scale=QLR ** -0.5,
                               accum_out=st[:, c:c + 1]).then_inc(sem("lat_squares"), 1)
            make_hi(act, MLA + 4)
            make_hi(act, MLA + 5)
            act.wait_ge(chunk_used, MLA + 4)
            for c in range(TC):
                act.activation(QB[:, c, 0:KVR], ps[:, 3 + c, 0:KVR], ACT.Square, scale=KVR ** -0.5,
                               accum_out=st[:, 3 + c:4 + c]).then_inc(sem("lat_squares"), 1)
            make_hi(act, MLA + 6)
            for k in range(4):
                act.wait_ge(sem("cq_turned"), k + 1)
                act.activation(cqf[:, k, :], ps[:, 6 + k % 2, 0:T], ACT.Copy,
                               scale=vT[:, QNG + k:QNG + k + 1]).then_inc(sem("cq_scaled"), 1)
            act.wait_ge(sem("ckv_made"), TC)
            act.wait_ge(sem("cache_in"), 32)
            act.activation(pT[:, 0, 0:KC * RD].rearrange("p (c r) -> p c r", c=KC), ckv[:, :, KVR:KVR + RD], ACT.Square)\
                .then_inc(sem("kr_square"), 1)

            def project(n, par, L):
                act.wait_ge(chunk_used, at(kv_chunk(n) + 1, L(3)))
                act.activation(KT[:, :, :].rearrange("p a b -> p (a b)").rearrange("p (c h r) -> p c h r", c=KC, h=2),
                               ps[:, 4:8, :].rearrange("p c (h r) -> p c h r", h=2)[:, :, :, 0:P],
                               ACT.Square).then_inc(sem("k_square"), 1)
                for dst, o in ((k_sb[:, :, :, :], 0), (v_sb[:, par, :, :, :], P)):
                    act.activation(dst, ps[:, 4:8, :].rearrange("p c (h r) -> p c h r", h=2)[:, :, :, o:o + P],
                                   ACT.Copy).then_inc(sem("k_copied"), 1)

            def queries(n, L, square):
                act.wait_ge(chunk_used, at(kv_chunk(n) + 2, L(3)))
                if square:
                    act.activation(QB[:, :, :], ps[:, 0:3, 0:384], ACT.Square).then_inc(sem("q_square"), 1)
                else:
                    act.activation(q_sb[:, :, :].rearrange("p a r -> p (a r)").rearrange("p (c n) -> p c n", c=TC),
                                   ps[:, 0:3, 0:384], ACT.Copy).then_inc(sem("q_copied"), 1)

            def turned(n, L):
                act.wait_ge(sem("k_turned"), at(n + 1, L(1)))
                act.activation(KT[:, :, :], ps[:, 6:8, :], ACT.Copy, scale=vT[:, KKG:KKG + 1]).then_inc(sem("kT_made"), 1)
                act.wait_ge(sem("q_turned"), at(n + 1, L(1)))
                for h in range(2):
                    act.activation(QB[:, h, :], ps[:, 1 + h, 0:T], ACT.Copy,
                                   scale=vT[:, QKG:QKG + 1]).then_inc(sem("kT_made"), 1)

            def attend(n, i, g=None, more=True):
                L = turns(g)
                for h in range(2):
                    for c in range(TC):
                        act.wait_ge(sem("max_made"), at(6 * n + 3 * h + max(c, 1) + 1, L(6)))
                        a, b = ((0, P), (P, 4 * P), (0, 3 * P))[c]
                        o = (0, P, 4 * P)[c]
                        act.activation(pr[:, h, o:o + b - a], ps[:, 2 * h + c // 2, a:b], ACT.Exp,
                                       bias=st[:, 40 + 3 * h + c:41 + 3 * h + c],
                                       accum_out=st[:, 48 + 3 * h + c:49 + 3 * h + c]).then_inc(sem("exp_made"), 1)
                if more:
                    project(n + 1, 1 - i, L)
                    make_hi(act, kv_chunk(n + 1) + 3, L(3))
                for h in range(2):
                    act.wait_ge(sem("p_turned"), at(2 * n + h + 1, L(2)))
                    act.activation(pT[:, h, 0:512], ps[:, 4 + 2 * h, :], ACT.Copy).then_inc(sem("pT_hi"), 1)
                for h in range(2):
                    if more:
                        queries(n + 1, L, h == 0)
                    act.wait_ge(sem("o_made"), at(2 * n + h + 1, L(2)))
                    act.activation(oTh[:, h, :], ps[:, 3 + h, 0:T], ACT.Copy).then_inc(sem("oT_hi"), 1)
                if more:
                    make_hi(act, kv_chunk(n + 1) + 4, L(3))
                    turned(n + 1, L)
                    make_hi(act, kv_chunk(n + 1) + 5, L(3))

            project(0, 0, turns())
            make_hi(act, GRP + 3)
            queries(0, turns(), True)
            queries(0, turns(), False)
            make_hi(act, GRP + 4)
            turned(0, turns())
            with act.Fori(0, NPAIR // 2 - 1) as g:
                attend(0, 0, g)
                attend(1, 1, g)
            attend(NPAIR - 2, 0)
            attend(NPAIR - 1, 1, more=False)

            norm_act(act, "moe", 1, 1, "mla_x", 0)
            act.wait_ge(sem("tok_turned"), 1)
            for c in range(TC):
                act.activation(xn[:, c, :], ps[:, 2 * c:2 * c + 2, :].rearrange("p a b -> p (a b)"), ACT.Copy)\
                    .then_inc(sem("tok_made"), 1)
            act.wait_ge(sem("gap_made"), 1)
            act.activation(rt[:, 9, :, 1:2], rt[:, 9, :, 0:1], ACT.Exp).then_inc(sem("gap_exp"), 1)

            def heads(t):
                for k in range(2):
                    make_hi(act, MOE + k, (t, TILE_CH))

            def tile(t, ahead=False):
                L = (t, TILE_CH)
                act.wait_ge(sem("gathered"), at(1, (t, 1)))
                act.activation(xgh[:, :, :].rearrange("p a b -> p (a b)"), ps[:, 4:6, :].rearrange("p a b -> p (a b)"),
                               ACT.Copy).then_inc(sem("xg_hi"), 1)
                make_hi(act, MOE + 2, L)
                for k in range(14 + 1):
                    if k in (1, 5, 9):
                        g = k // 4
                        act.wait_ge(chunk_used, at(MOE + k + 1, L))
                        act.wait_ge(sem("hm_made"), at(g + 1, (t, 3)))
                        act.activation(ms[:, :], ps[:, 2 * (g % 2), :], ACT.Silu).then_inc(sem("ms_made"), 1)
                    if k in (5, 9, 13):
                        g = k // 4 - 1
                        act.wait_ge(sem("hm_turned"), at(g + 1, (t, 3)))
                        act.activation(hgh[:, 4 * g:4 * g + 4, :].rearrange("p a b -> p (a b)"), ps[:, 5 - g % 2, :],
                                       ACT.Copy).then_inc(sem("hg_hi"), 1)
                    make_hi(act, MOE + k + 3, L)
                    if k == 0:
                        act.wait_ge(sem("sel_turned"), at(1, (t, 1)))
                        act.activation(selT[:, :], ps[:, 4, 0:T], ACT.Copy).then_inc(sem("selT_made"), 1)
                if ahead:
                    heads(t + 1)
                act.wait_ge(chunk_used, at(MOE + TILE_CH, L))
                act.activation(yh[:, :], ps[:, 6:8, :].rearrange("p a b -> p (a b)"), ACT.Copy).then_inc(sem("y_hi"), 1)

            act.wait_ge(sem("moe_const"), 10)
            with act.Fori(0, NE - 1) as e:
                tile(e, True)
            tile(NE - 1)
            act.wait_ge(sem("tab_ready"), 1)
            more = act.value_load(tab[0:1, 0:1], min_val=0, max_val=NX)
            with act.Fori(0, NX) as j:
                with act.If(j < more):
                    heads(j + NE)
                    tile(j + NE)

        @block.vector
        def _(dve):
            step = Steps(dve, sem("dve_steps"))
            dve.wait_ge(sem("ident_made"), 1)
            dve.wait_ge(sem("vec_turned"), 1)
            dve.tensor_copy(dwT[:, 0:P], ps[:, 7, P:2 * P]).then_inc(sem("dw_made"), 1)
            dve.tensor_copy(dwT[:, P:CW * DK], ps[:, 7, 2 * P:P + CW * DK]).then_inc(sem("dw_made"), 1)
            dve.tensor_copy(vT[:, :], ps[:, 7, 0:64]).then_inc(sem("vT_made"), 1)

            def modulation(layer):
                dve.wait_ge(sem(f"rows_turned{layer}"), 1)
                step(dve.tensor_copy(mT[:, :, :], ps[:, 3, 0:256].rearrange("p (m r) -> p m r", r=8)[:, :, 0:3]))
                for cond in range(2):
                    m = modv[:, layer, cond, :, :].rearrange("p a b -> p (a b)")
                    step(dve.tensor_tensor(m, mT[:, :, cond], mT[:, :, 2], ALU.add))
                for n, g0 in ((0, N1G), (1, N2G)):
                    for cond in range(2):
                        step(dve.scalar_tensor_tensor(
                            out=modA[:, layer, n, cond, :], in0=modv[:, layer, cond, 2 * n + 1, :], scalar=1.0,
                            in1=vT[:, g0 + DK * layer:g0 + DK * layer + DK], op0=ALU.add, op1=ALU.mult))
                dve.tensor_copy(st[:, 63:64], ones[:, 0:1]).then_inc(sem(f"mod_ready{layer}"), 1)

            dve.wait_ge(sem("ones_made"), 2)
            modulation(0)
            for s in range(3):
                make_lo(dve, PW1 + s)
            norm_dve(dve, step, "conv")
            split_dve(dve, "conv", "conv_modulated", 2)
            dve.wait_ge(sem("u_zero"), 1)
            for t in range(4):
                if t < 3:
                    make_lo(dve, PW1 + 2 * t + 3)
                dve.wait_ge(sem("sig_made"), t + 1)
                b = 4 * (t % 2)
                for a, e, o in ((0, P, PAD), (P, T, 2 * PAD)):
                    dve.tensor_tensor(u[:, 2 * t:2 * t + 2, a + o:e + o], ps[:, b:b + 2, a:e], sig[:, t % 2, :, a:e],
                                      ALU.mult).then_inc(sem("glu_done"), 1)
                if t < 2:
                    make_lo(dve, PW1 + 2 * t + 4)
            dve.wait_ge(sem("glu_done"), 8)
            dve.wait_ge(sem("dw_made"), 2)
            taps = sem("dve_taps")
            for j in range(DVE_BLOCKS):
                dve.tensor_scalar(v[:, j, :], u[:, j, 0:CV], dwT[:, j:j + 1], vT[:, DWB + j:DWB + j + 1],
                                  ALU.mult, ALU.add).then_inc(taps, 1)
            with dve.Fori(0, (CW - 1) // TAPS) as it:
                for w in range(1, TAPS + 1):
                    for j in range(DVE_BLOCKS):
                        dve.wait_ge(taps, at(DVE_BLOCKS * (w - 1) + j + 1, (it, DVE_BLOCKS * TAPS)))
                        dve.scalar_tensor_tensor(out=v[:, j, :], in0=u[:, j, ds(it * TAPS + w, CV)],
                                                 scalar=dwT[:, ds(it * TAPS * DK + w * DK + j, 1)],
                                                 in1=v[:, j, :], op0=ALU.mult, op1=ALU.add).then_inc(taps, 1)
            modulation(1)
            dve.wait_ge(sem("ln_mean"), 1)
            dve.wait_ge(sem("dve_taps"), DVE_BLOCKS * CW)
            dve.wait_ge(sem("pool_taps"), REST * (CW - 1))
            for j in range(DK):
                dve.scalar_tensor_tensor(out=v[:, j, :], in0=ps[:, 0, 0:CV], scalar=-1.0 / D, in1=v[:, j, :],
                                         op0=ALU.mult, op1=ALU.add).then_inc(sem("ln_centred"), 1)
            for s in range(3):
                make_lo(dve, PW2 + s)
            dve.wait_ge(sem("ln_root"), 1)
            step(dve.reciprocal(rs[:, :], sd[:, :]))
            dve.wait_ge(sem("ln_centred"), DK)
            for j in range(DK):
                dve.tensor_tensor(v[:, j, :], v[:, j, :], rs[:, :], ALU.mult).then_inc(sem("ln_scaled"), 1)
            split_dve(dve, "ln", "ln_done", 2)
            for q in range(DK // 2):
                make_lo(dve, PW2 + q + 3)
            dve.wait_ge(chunk_used, PW2 + 4)
            dve.wait_ge(sem("gate_in"), 32)
            residual(dve, step, "conv", lambda c: ps[:, 2 * c:2 * c + 2, :].rearrange("p a b -> p (a b)"))

            norm_dve(dve, step, "ffn")
            dve.wait_ge(sem("gates_out1"), 16)
            split_dve(dve, "ffn", "ffn_modulated", 2)

            def hidden(b, value, loop, up, free):
                dve.wait_ge(sem("ffn_silu"), at(value, loop))
                dve.wait_ge(*up)
                if free:
                    dve.wait_ge(*free)
                dve.tensor_tensor(ff[:, b, :], ps[:, 7, 0:T], fs[:, b, :], ALU.mult).then_inc(sem("ffn_prod"), 1)
                dve.wait_ge(sem("ffn_prod"), at(value, loop))
                dve.tensor_copy(fh[:, b, :], ff[:, b, :]).then_inc(sem("ffn_hi"), 1)
                dve.wait_ge(sem("ffn_hi"), at(value, loop))
                dve.tensor_tensor(fl[:, b, :], ff[:, b, :], fh[:, b, :], ALU.subtract).then_inc(sem("ffn_lo"), 1)

            up, down = sem("ffn_up"), sem("ffn_down")
            hidden(0, 1, None, (up, 2), None)
            hidden(1, 2, None, (chunk_used, FFN + 2), None)
            make_lo(dve, FFN + 3)
            make_lo(dve, FFN + 4)
            hidden(0, 3, None, (up, 4), (down, 1))
            make_lo(dve, FFN + 5)
            with dve.Fori(0, 4) as it:
                for i in (1, 2):
                    hidden(1, 2 * i + 2, (it, 4), (chunk_used, at(FFN + 3 * i + 2, (it, 6))), None)
                    make_lo(dve, FFN + 3 * i + 3, (it, 6))
                    make_lo(dve, FFN + 3 * i + 4, (it, 6))
                    hidden(0, 2 * i + 3, (it, 4), (up, at(2 * i + 4, (it, 4))), (down, at(i + 1, (it, 2))))
                    make_lo(dve, FFN + 3 * i + 5, (it, 6))
            hidden(1, 20, None, (chunk_used, FFN + 29), None)
            make_lo(dve, FFN + 30)
            make_lo(dve, FFN + 31)
            hidden(0, 21, None, (up, 22), (down, 10))
            make_lo(dve, FFN + 32)
            hidden(1, 22, None, (chunk_used, FFN + 32), None)
            for i in range(3):
                make_lo(dve, MLA + i)
            dve.wait_ge(chunk_used, FFN + 33)
            dve.wait_ge(sem("gate_in"), 64)
            residual(dve, step, "ffn", lambda c: ps[:, 2 * c:2 * c + 2, :].rearrange("p a b -> p (a b)"))

            norm_dve(dve, step, "mla")
            split_dve(dve, "mla", "mla_modulated", 2)
            make_lo(dve, MLA + 3)
            dve.wait_ge(sem("lat_squares"), TC)
            rsqrt(step, st[:, 6:9], st[:, 0:3], TC)
            for c in range(TC):
                dve.tensor_scalar(xn[:, c, 0:QLR], ps[:, c, :], st[:, 6 + c:7 + c], None, ALU.mult).then_inc(sem("cq_made"), 1)
            dve.wait_ge(sem("lat_squares"), 2 * TC)
            rsqrt(step, st[:, 9:12], st[:, 3:6], TC)
            for c in range(TC):
                step(dve.tensor_copy(ckv[:, c, KVR:KVR + RD], ps[:, 3 + c, KVR:KVR + RD]))
                step(dve.tensor_scalar(ckv[:, c, 0:KVR], ps[:, 3 + c, 0:KVR], st[:, 9 + c:10 + c], None, ALU.mult))
            dve.wait_ge(sem("tk_in"), 5 * 16)
            for c in range(TC):
                dve.tensor_tensor(ckv[:, c, 0:KVR], ckv[:, c, 0:KVR], gb[:, 2 * RD:2 * RD + KVR],
                                  ALU.mult).then_inc(sem("ckv_made"), 1)
            dve.wait_ge(sem("tq_in"), 4 * 16)

            def by_half(t):
                w = t.rearrange("p n (a h r) -> p n a h r", a=2, h=2)
                return w[:, :, :, 0, :], w[:, :, :, 1, :]

            for tab_, g0, n in ((tk, RD, KC), (tq, 0, 2 * TC)):
                g = gb[:, g0:g0 + RD]
                step(dve.tensor_tensor(tab_[:, 0, :, :], tab_[:, 0, :, :], g.unsqueeze(1).to_broadcast([P, n, RD]), ALU.mult))
                s = by_half(tab_[:, 1, :, :])
                gh = by_half(g.unsqueeze(1).to_broadcast([P, n, RD]))
                for h in range(2):
                    step(dve.tensor_tensor(s[h], s[h], gh[1 - h], ALU.mult))

            def rotate(dst, tmp, src, tab_):
                step(dve.tensor_tensor(dst, src, tab_[:, 0, :, :], ALU.mult))
                a, b, s = by_half(tmp), by_half(src), by_half(tab_[:, 1, :, :])
                for h in range(2):
                    step(dve.tensor_tensor(a[h], b[1 - h], s[h], ALU.mult))

            dve.wait_ge(sem("ckv_made"), TC)
            dve.wait_ge(sem("cache_in"), 32)
            dve.wait_ge(sem("kr_square"), 1)
            step(dve.tensor_reduce(st[:, 12:16], pT[:, 0, 0:KC * RD].rearrange("p (c r) -> p c r", c=KC), AX, ALU.add))
            qrt = qr[:, 0, 0:KC, :]
            rotate(kr_rot[:, :, :], qrt, ckv[:, :, KVR:KVR + RD], tk)
            dve.tensor_tensor(kr_rot[:, :, :], kr_rot[:, :, :], qrt, ALU.add).then_inc(sem("kr_ready"), 1)
            for k in range(4):
                dve.wait_ge(sem("cq_scaled"), k + 1)
                step(dve.tensor_copy(cqTh[:, k, :], cqf[:, k, :]))
                step(dve.tensor_tensor(cqTl[:, k, :], cqf[:, k, :], cqTh[:, k, :], ALU.subtract))
            for k in range(2):
                dve.wait_ge(sem("ck_turned"), k + 1)
                dve.tensor_copy(ckTh[:, k, :], ps[:, k, :]).then_inc(sem("lat_split"), 1)
                dve.wait_ge(sem("lat_split"), 2 * k + 1)
                dve.tensor_tensor(ckTl[:, k, :], ps[:, k, :], ckTh[:, k, :], ALU.subtract).then_inc(sem("lat_split"), 1)
            dve.wait_ge(sem("yacc_zero"), 1)
            dve.sem_inc(sem("att_y"), 1)

            def keys(n, L):
                dve.wait_ge(sem("k_square"), at(n + 1, L(1)))
                step(dve.tensor_reduce(st[:, 16:24], KT[:, :, :].rearrange("p a b -> p (a b)")
                                       .rearrange("p (c r) -> p c r", r=P), AX, ALU.add))
                step(dve.tensor_tensor(st[:, 16:24].rearrange("p (c h) -> p c h", h=2),
                                       st[:, 16:24].rearrange("p (c h) -> p c h", h=2),
                                       st[:, 12:16].unsqueeze(2).to_broadcast([P, KC, 2]), ALU.add))
                step(dve.tensor_scalar(st[:, 16:24], st[:, 16:24], 1.0 / QKD, None, ALU.mult))
                rsqrt(step, st[:, 24:32], st[:, 16:24], 8)
                dve.wait_ge(sem("k_copied"), at(2 * n + 2, L(2)))
                rk = st[:, 24:32].rearrange("p (c h) -> p c h", h=2)
                step(dve.tensor_tensor(k_sb[:, :, :, :], k_sb[:, :, :, :], rk.unsqueeze(3).to_broadcast([P, KC, 2, P]), ALU.mult))
                dve.tensor_tensor(krh[:, :, :, :], kr_rot[:, :, :].unsqueeze(2).to_broadcast([P, KC, 2, RD]),
                                  rk.unsqueeze(3).to_broadcast([P, KC, 2, RD]), ALU.mult).then_inc(sem("k_scaled"), 1)

            def queries(n, L):
                dve.wait_ge(sem("q_square"), at(n + 1, L(1)))
                step(dve.tensor_reduce(st[:, 32:38], QB[:, :, :].rearrange("p a b -> p (a b)")
                                       .rearrange("p (c r) -> p c r", r=QKD), AX, ALU.add))
                step(dve.tensor_scalar(st[:, 32:38], st[:, 32:38], 1.0 / QKD, None, ALU.mult))
                rsqrt(step, st[:, 56:62], st[:, 32:38], 6)
                step(dve.tensor_scalar(st[:, 56:62], st[:, 56:62], QKD ** -0.5, None, ALU.mult))
                dve.wait_ge(sem("q_copied"), at(n + 1, L(1)))
                step(dve.tensor_tensor(q_sb[:, :, :], q_sb[:, :, :],
                                       st[:, 56:62].unsqueeze(2).to_broadcast([P, 2 * TC, QKD]), ALU.mult))
                rotate(qr[:, 0, :, :], qr[:, 1, :, :], q_sb[:, :, P:QKD], tq)
                dve.tensor_tensor(qr[:, 0, :, :], qr[:, 0, :, :], qr[:, 1, :, :], ALU.add).then_inc(sem("q_scaled"), 1)

            def turned(n, L):
                dve.wait_ge(sem("k_turned"), at(n + 1, L(1)))
                dve.tensor_copy(KR[:, :], ps[:, 0, :]).then_inc(sem("rT_made"), 1)
                dve.wait_ge(sem("q_turned"), at(n + 1, L(1)))
                dve.tensor_copy(QB[:, 2, :], ps[:, 3, 0:T]).then_inc(sem("rT_made"), 1)

            def attend(n, g=None, more=True):
                L = turns(g)
                out_chunk = kv_chunk(n + 1) + 2

                def add_out(c):
                    if c < 2:
                        dve.wait_ge(sem("out_made"), at(2 * n + c + 1, L(2)))
                    else:
                        dve.wait_ge(chunk_used, at((out_chunk if more else MOE - 1) + 1, L(3)))
                    dve.tensor_tensor(yacc[:, c, :], yacc[:, c, :],
                                      ps[:, 2 * c:2 * c + 2, :].rearrange("p a b -> p (a b)"), ALU.add).then_inc(sem("att_y"), 1)

                for h in range(2):
                    dve.wait_ge(sem("scored"), at(2 * n + h + 1, L(2)))
                    for c in range(TC):
                        a, b = ((0, P), (P, 4 * P), (0, 3 * P))[c]
                        dve.tensor_reduce(st[:, 40 + 3 * h + c:41 + 3 * h + c], ps[:, 2 * h + c // 2, a:b], AX, ALU.max,
                                          negate=True).then_inc(sem("max_made"), 1)
                for h in range(2):
                    dve.wait_ge(sem("exp_made"), at(6 * n + 3 * h + 3, L(6)))
                    step(dve.reciprocal(st[:, 3 * h:3 * h + 3], st[:, 48 + 3 * h:51 + 3 * h]))
                    for c in range(TC):
                        o, e = ((0, P), (P, 4 * P), (4 * P, 7 * P))[c]
                        dve.tensor_scalar(pr[:, h, o:e], pr[:, h, o:e], st[:, 3 * h + c:3 * h + c + 1], None,
                                          ALU.mult).then_inc(sem("p_made"), 1)
                if more:
                    keys(n + 1, L)
                for h in range(2):
                    dve.wait_ge(sem("p_turned"), at(2 * n + h + 1, L(2)))
                    dve.tensor_copy(pT[:, h, 512:7 * P], ps[:, 5 + 2 * h, 0:T]).then_inc(sem("pT_lo"), 1)
                if more:
                    make_lo(dve, out_chunk, L(3))
                else:
                    make_lo(dve, MOE + 1)
                for h in range(2):
                    dve.wait_ge(sem("oT_hi"), at(2 * n + h + 1, L(2)))
                    dve.tensor_tensor(oTl[:, h, :], ps[:, 3 + h, 0:T], oTh[:, h, :], ALU.subtract).then_inc(sem("oT_lo"), 1)
                if more:
                    make_lo(dve, out_chunk + 1, L(3))
                    queries(n + 1, L)
                for c in range(TC):
                    add_out(c)
                if more:
                    turned(n + 1, L)
                    make_lo(dve, out_chunk + 2, L(3))

            keys(0, turns())
            dve.wait_ge(lo_made, split_no(GRP + 3))
            make_lo(dve, GRP + 3)
            queries(0, turns())
            turned(0, turns())
            with dve.Fori(0, NPAIR // 2 - 1) as g:
                step.begin(g, 2 * (2 * RSQRT_STEPS + 13))
                attend(0, g)
                attend(1, g)
                step.end(NPAIR // 2 - 1)
            attend(NPAIR - 2)
            attend(NPAIR - 1, more=False)
            dve.wait_ge(sem("att_y"), TC * NPAIR + 1)
            dve.wait_ge(sem("gate_in"), 96)
            residual(dve, step, "mla", lambda c: yacc[:, c, :])

            norm_dve(dve, step, "moe")
            dve.wait_ge(sem("moe_const"), 10)
            dve.wait_ge(sem("logit_rows"), 1)
            dve.tensor_copy(lgT[:, :], ps[0:NE, 5, 0:T]).then_inc(sem("logit_copied"), 1)
            dve.wait_ge(sem("logits_made"), 1)
            L, W, O1, O2, L2, GT, M, TMP = (rt[:, i, :, :] for i in range(8))
            stt = rt[:, 8, :, :]
            gap = rt[:, 9, :, :]
            rev = rt[:, 10, :, :]
            wide = [P, TC, NE]

            def one(t, i):
                return t[:, :, i:i + 1].to_broadcast(wide)

            step(dve.tensor_copy(L, ps[:, 6, 0:TC * NE].rearrange("p (c e) -> p c e", c=TC)))
            for c in range(TC):
                step(dve.tensor_scalar(rev[:, c, :], iota[:, 0:NE], -1.0, float(NE), ALU.mult, ALU.add))

            def best(src, oh, m):
                step(dve.tensor_reduce(stt[:, :, m:m + 1], src, AX, ALU.max))
                step(dve.tensor_tensor(W, src, one(stt, m), ALU.is_equal))
                step(dve.tensor_tensor(W, W, rev, ALU.mult))
                step(dve.tensor_reduce(stt[:, :, m + 1:m + 2], W, AX, ALU.max))
                step(dve.tensor_tensor(oh, W, one(stt, m + 1), ALU.is_equal))

            best(L, O1, 0)
            step(dve.scalar_tensor_tensor(out=L2, in0=O1, scalar=GONE, in1=L, op0=ALU.mult, op1=ALU.add))
            best(L2, O2, 2)
            step(dve.tensor_tensor(M, O1, O2, ALU.add))
            dve.tensor_tensor(gap[:, :, 0:1], stt[:, :, 2:3], stt[:, :, 0:1], ALU.subtract).then_inc(sem("gap_made"), 1)
            dve.wait_ge(sem("gap_exp"), 1)
            step(dve.tensor_scalar(gap[:, :, 2:3], gap[:, :, 1:2], 1.0, None, ALU.add))
            step(dve.reciprocal(gap[:, :, 3:4], gap[:, :, 2:3]))
            step(dve.tensor_tensor(gap[:, :, 4:5], gap[:, :, 1:2], gap[:, :, 3:4], ALU.mult))
            step(dve.tensor_tensor(GT, O1, one(gap, 3), ALU.mult))
            step(dve.tensor_tensor(TMP, O2, one(gap, 4), ALU.mult))
            step(dve.tensor_tensor(GT, GT, TMP, ALU.add))
            step(dve.tensor_copy(G[:, :, 1:NE + 1], GT))
            dve.wait_ge(sem("ranked"), 1)
            rk = ps[:, 7, 0:TC * NE].rearrange("p (c e) -> p c e", c=TC)
            step(dve.scalar_tensor_tensor(out=TMP, in0=rk, scalar=BIG, in1=M, op0=ALU.add, op1=ALU.mult))
            step(dve.tensor_scalar(R[:, :, 0:NE], TMP, -BIG, None, ALU.add))

            def make_sel(t):
                for c in range(TC):
                    dve.tensor_scalar(sel[:, c, :], iota[:, :], R[:, c, t], None, ALU.is_equal).then_inc(sem("sel_made"), 1)

            make_sel(slice(0, 1))
            cnt, ex, cum, cux = (jt[:, i, :] for i in range(4))
            dve.wait_ge(sem("counted"), 1)
            step(dve.tensor_copy(cnt, ps[:, 6, TC * NE:TC * NE + NE]))
            step(dve.tensor_scalar(ex, cnt, float(P), None, ALU.is_gt))
            for b in range(2, TC):
                step(dve.scalar_tensor_tensor(out=ex, in0=cnt, scalar=float(b * P), in1=ex, op0=ALU.is_gt, op1=ALU.add))
            step(dve.tensor_tensor(upto[:, :, :], upto[:, :, :], ex.unsqueeze(1).to_broadcast([P, NE, NE]), ALU.mult))
            step(dve.tensor_reduce(cum, upto[:, :, :], AX, ALU.add))
            step(dve.tensor_tensor(cux, cum, ex, ALU.subtract))
            step(dve.memset(R[:, :, NE:NT], -BIG))
            step(dve.memset(G[:, :, NE + 1:NT + 1], 0.0))
            has, to, w = xj[:, 0, :, :], xj[:, 1, :, :], xj[:, 2, :, :]
            over = [P, NX, NE]
            step(dve.tensor_tensor(w, cum.unsqueeze(1).to_broadcast(over), js[:, :, :], ALU.is_gt))
            step(dve.tensor_tensor(to, cux.unsqueeze(1).to_broadcast(over), js[:, :, :], ALU.subtract))
            step(dve.scalar_tensor_tensor(out=has, in0=to, scalar=0.0, in1=w, op0=ALU.is_le, op1=ALU.mult))
            step(dve.tensor_scalar(to, to, float(P), float(BIG - P), ALU.mult, ALU.add))
            all_ = [P, TC, NX, NE]
            by_token, by_tile = (lambda t: t.unsqueeze(2).to_broadcast(all_)), (lambda t: t.unsqueeze(1).to_broadcast(all_))
            step(dve.tensor_tensor(xw[:, :, :, :], by_token(R[:, :, 0:NE]), by_tile(to), ALU.add))
            step(dve.tensor_tensor(xw[:, :, :, :], xw[:, :, :, :], by_tile(has), ALU.mult))
            step(dve.tensor_reduce(R[:, :, NE:NE + NX], xw[:, :, :, :], AX, ALU.add))
            step(dve.tensor_scalar(R[:, :, NE:NE + NX], R[:, :, NE:NE + NX], -BIG, None, ALU.add))
            step(dve.tensor_tensor(xw[:, :, :, :], by_token(GT), by_tile(has), ALU.mult))
            step(dve.tensor_reduce(G[:, :, NE + 1:NE + 1 + NX], xw[:, :, :, :], AX, ALU.add))
            ids = jt[:, 4, :]
            step(dve.tensor_copy(ids[:, 0:1], cum[:, NE - 1:NE]))
            step(dve.tensor_tensor(w, has, iota[:, 0:NE].unsqueeze(1).to_broadcast(over), ALU.mult))
            step(dve.tensor_reduce(ids[:, 1:NX + 1], w, AX, ALU.add))
            dve.tensor_copy(tab[0:1, 0:NX + 1], ids[0:1, 0:NX + 1]).then_inc(sem("tab_ready"), 1)
            dve.sem_inc(sem("hm_made"), 1)
            dve.sem_inc(sem("y_lo"), 1)
            dve.wait_ge(sem("yacc_zero"), 2)

            def heads(t):
                for k in range(2):
                    make_lo(dve, MOE + k, (t, TILE_CH))

            def add_scattered(c, t, value):
                b = (0, 2, 6)[c]
                dve.wait_ge(sem("scattered"), value)
                dve.scalar_tensor_tensor(out=yacc[:, c, :], in0=ps[:, b:b + 2, :].rearrange("p a b -> p (a b)"),
                                         scalar=G[:, c, t], in1=yacc[:, c, :], op0=ALU.mult, op1=ALU.add)\
                    .then_inc(sem("y_added"), 1)

            def tile(t, ahead=False):
                L = (t, TILE_CH)
                tt = ds(t, 1)
                dve.wait_ge(sem("xg_hi"), at(1, (t, 1)))
                dve.tensor_tensor(xgl[:, :, :].rearrange("p a b -> p (a b)"), ps[:, 4:6, :].rearrange("p a b -> p (a b)"),
                                  xgh[:, :, :].rearrange("p a b -> p (a b)"), ALU.subtract).then_inc(sem("xg_lo"), 1)
                add_scattered(0, tt, at(1, (t, 3)))
                make_lo(dve, MOE + 2, L)
                add_scattered(1, tt, at(2, (t, 3)))
                make_lo(dve, MOE + 3, L)
                add_scattered(2, tt, at(3, (t, 3)))
                for k in range(1, 15):
                    if k in (3, 7, 11):
                        g = k // 4
                        dve.wait_ge(sem("ms_made"), at(g + 1, (t, 3)))
                        dve.wait_ge(chunk_used, at(MOE + k + 1, L))
                        dve.tensor_tensor(hm[:, g % 2, :], ps[:, 2 * (g % 2) + 1, :], ms[:, :], ALU.mult).then_inc(sem("hm_made"), 1)
                    if k in (5, 9, 13):
                        g = k // 4 - 1
                        dve.wait_ge(sem("hg_hi"), at(g + 1, (t, 3)))
                        dve.tensor_tensor(hgl[:, 4 * g:4 * g + 4, :].rearrange("p a b -> p (a b)"), ps[:, 5 - g % 2, :],
                                          hgh[:, 4 * g:4 * g + 4, :].rearrange("p a b -> p (a b)"),
                                          ALU.subtract).then_inc(sem("hg_lo"), 1)
                    make_lo(dve, MOE + k + 3, L)
                    if k == 8:
                        dve.wait_ge(sem("sel_turned"), at(1, (t, 1)))
                        make_sel(ds(t + 1, 1))
                if ahead:
                    heads(t + 1)
                dve.wait_ge(sem("y_hi"), at(1, (t, 1)))
                dve.tensor_tensor(yl[:, :], ps[:, 6:8, :].rearrange("p a b -> p (a b)"), yh[:, :],
                                  ALU.subtract).then_inc(sem("y_lo"), 1)

            with dve.Fori(0, NE - 1) as e:
                tile(e, True)
            tile(NE - 1)
            more = dve.value_load(tab[0:1, 0:1], min_val=0, max_val=NX)
            with dve.Fori(0, NX) as j:
                with dve.If(j < more):
                    heads(j + NE)
                    tile(j + NE)
            last = more + NE
            for c in range(TC):
                add_scattered(c, ds(last, 1), at(c + 1, (last, 3)))
            dve.wait_ge(sem("y_added"), at(3, (last, 3)))
            dve.wait_ge(sem("gate_in"), 128)
            residual(dve, step, "moe", lambda c: yacc[:, c, :])

        @block.tensor
        def _(pe):
            pe.wait_ge(sem("ident_made"), 1)
            pe.wait_ge(sem("cond_in"), 32)
            pe.transpose(ps[:, 7, 0:2 * DK], cnd[:, :], ident[0:2 * DK, 0:2 * DK]).then_inc(sem("cond_turned"), 1)
            pe.wait_ge(sem("cst_made"), 1)

            def turn_vectors():
                pe.wait_ge(sem("vec_in"), 16 * 12)
                pe.transpose(ps[:, 7, 0:64], vec[0:64, 0, :], ident[0:64, 0:64])
                pe.transpose(ps[:, 7, P:2 * P], vec[:, 1, :], ident[:, :])
                n = CW * DK - P
                pe.transpose(ps[:, 7, 2 * P:2 * P + n], vec[0:n, 2, :], ident[0:n, 0:n]).then_inc(sem("vec_turned"), 1)

            def ada(layer, base):
                with pe.Fori(0, 4) as it:
                    for k in range(6):
                        if k % 2 == 0:
                            pe.wait_ge(sem(f"ada_row{layer}"), at(k // 2 + 1, (it, 3)))
                        slot = (base + k) % RAW
                        pe.wait_ge(raw_in[slot], at(16 * ((base + k) // RAW + 1), (it, 16)))
                        w = as_rows(512, 4)(raw[:, slot, :])
                        for i in range(4):
                            kk = 4 * (k % 2) + i
                            last = pe.matmul(ps[0:2, k // 2, :], cst[:, kk, :], w[:, i, :], start=kk == 0, stop=kk == DK - 1)
                        last.then_inc(chunk_used, 1)
                if layer == 0:
                    turn_vectors()
                pe.wait_ge(sem(f"ada_row{layer}"), 3 + 12)
                pe.wait_ge(sem(f"bias_in{layer}"), 16)
                for i in range(32):
                    m = (0, 1, 3, 4)[i // DK]
                    last = pe.transpose(ps[:, 3, 8 * i:8 * i + 3], mrow[0:3, m * D + (i % DK) * P:m * D + (i % DK + 1) * P],
                                        ident[0:3, 0:3])
                last.then_inc(sem(f"rows_turned{layer}"), 1)
                if layer == 0:
                    pe.wait_ge(sem("vT_made"), 1)
                for i in range(4):
                    c0 = (2, 5)[i // 2] * D + i % 2 * 512
                    last = pe.matmul(ps[0:2, 4 + i, :], comb[:, :], mrow[0:3, c0:c0 + 512], start=True, stop=True)
                last.then_inc(sem(f"gate_rows{layer}"), 1)

            ada(0, 0)
            pe.wait_ge(sem("grow_made0"), 1)
            norm_pe(pe, "conv")
            for t in range(4):
                for i in range(2):
                    s = PW1 + 2 * t + i
                    wait_parts(pe, s)
                    hi, lo = parts(s, 256, DK)
                    for m in range(2):
                        if t >= 2:
                            pe.wait_ge(sem("glu_done"), 2 * (t - 1))
                        b = 4 * (t % 2) + 2 * i + m
                        for k in range(DK):
                            if t == 0 and i == 0 and m == 0:
                                pe.wait_ge(sem("conv_h_lo"), k + 1)
                            last = mm3(ps[:, b, 0:T], hi[:, k, m * P:(m + 1) * P], lo[:, k, m * P:(m + 1) * P],
                                       hTh[:, k, :], hTl[:, k, :], k == 0, k == DK - 1)
                    last.then_inc(chunk_used, 1)
            pe.wait_ge(sem("glu_done"), 8)
            ada(1, ADA1)
            pe.wait_ge(sem("ones_made"), 2)
            for j in range(DK):
                if j < DVE_BLOCKS:
                    pe.wait_ge(sem("dve_taps"), DVE_BLOCKS * (CW - 1) + j + 1)
                else:
                    pe.wait_ge(sem("pool_taps"), REST * (CW - 2) + j - DVE_BLOCKS + 1)
                last = pe.matmul(ps[:, 0, 0:CV], ones[:, :], v[:, j, :], start=j == 0, stop=j == DK - 1)
            last.then_inc(sem("ln_mean"), 1)
            for j in range(DK):
                pe.wait_ge(sem("ln_square"), j + 1)
                pe.matmul(ps[:, 1, 0:CV], ones[:, :], sq[:, j % 2, :], start=j == 0, stop=j == DK - 1)\
                    .then_inc(sem("ln_summed"), 1)

            def rows_product(s, q, h_lo, first, blocks):
                wait_parts(pe, s)
                hi, lo = parts(s, D, 2)
                for i in range(2):
                    k = 2 * q + i
                    pe.wait_ge(sem(h_lo), k + 1)
                    for c in range(TC):
                        for h in range(2):
                            last = mm3(ps[:, 2 * c + h, :], hTh[:, k, c * P:(c + 1) * P], hTl[:, k, c * P:(c + 1) * P],
                                       hi[:, i, h * 512:(h + 1) * 512], lo[:, i, h * 512:(h + 1) * 512],
                                       k == 0, k == blocks - 1)
                last.then_inc(chunk_used, 1)

            pe.wait_ge(sem("ln_root"), 1)
            for q in range(DK // 2):
                rows_product(PW2 + q, q, "ln_h_lo", q == 0, DK)

            norm_pe(pe, "ffn")

            def ffn_up(s, sub, silus, prods, ends, first=False, loop=None):
                for i, (bank, name, need) in enumerate(((6, "ffn_silu", silus), (7, "ffn_prod", prods))):
                    wait_parts(pe, s + i, loop)
                    if not first:
                        pe.wait_ge(sem(name), need)
                    hi, lo = parts(s + i, 256, DK)
                    if first:
                        pe.wait_ge(sem("ffn_modulated"), 2 * (DK - 1 + i))
                    for k in range(DK):
                        if first and i == 0:
                            pe.wait_ge(sem("ffn_h_lo"), k + 1)
                        last = mm3(ps[:, bank, 0:T], hi[:, k, sub * P:(sub + 1) * P], lo[:, k, sub * P:(sub + 1) * P],
                                   hTh[:, k, :], hTl[:, k, :], k == 0, k == DK - 1)
                    last.then_inc(ends, 1)

            def ffn_down(s, sub, made, ends, first=False, final=False, loop=None):
                wait_parts(pe, s, loop)
                pe.wait_ge(sem("ffn_lo"), made)
                hi, lo = parts(s, D, 2)
                for c in range(TC):
                    for h in range(2):
                        last = mm3(ps[:, 2 * c + h, :], fh[:, sub, c * P:(c + 1) * P], fl[:, sub, c * P:(c + 1) * P],
                                   hi[:, sub, h * 512:(h + 1) * 512], lo[:, sub, h * 512:(h + 1) * 512], first, final)
                last.then_inc(ends, 1)

            up, down = sem("ffn_up"), sem("ffn_down")
            pe.wait_ge(sem("conv_x"), TC)
            ffn_up(FFN, 0, 0, 0, up, first=True)
            ffn_up(FFN, 1, 1, 1, chunk_used)
            ffn_down(FFN + 2, 0, 1, down, first=True)
            ffn_up(FFN + 3, 0, 2, 2, up)
            ffn_down(FFN + 2, 1, 2, chunk_used)
            with pe.Fori(0, 4) as it:
                for i in (1, 2):
                    s = FFN + 3 * i
                    ffn_up(s, 1, at(2 * i + 1, (it, 4)), at(2 * i + 1, (it, 4)), chunk_used, loop=(it, 6))
                    ffn_down(s + 2, 0, at(2 * i + 1, (it, 4)), down, loop=(it, 6))
                    ffn_up(s + 3, 0, at(2 * i + 2, (it, 4)), at(2 * i + 2, (it, 4)), up, loop=(it, 6))
                    ffn_down(s + 2, 1, at(2 * i + 2, (it, 4)), chunk_used, loop=(it, 6))
            s = FFN + 27
            ffn_up(s, 1, 19, 19, chunk_used)
            ffn_down(s + 2, 0, 19, down)
            ffn_up(s + 3, 0, 20, 20, up)
            ffn_down(s + 2, 1, 20, chunk_used)
            ffn_up(s + 3, 1, 21, 21, chunk_used)
            ffn_down(s + 5, 0, 21, down)
            ffn_down(s + 5, 1, 22, chunk_used, final=True)

            norm_pe(pe, "mla")
            pe.wait_ge(sem("ffn_x"), TC)
            for n, width, b in ((0, QLR, 0), (2, KVR + RD, 3)):
                for i in range(2):
                    s = MLA + n + i
                    wait_parts(pe, s)
                    hi, lo = parts(s, width, 4)
                    for kk in range(4):
                        k = 4 * i + kk
                        pe.wait_ge(sem("mla_h_lo"), k + 1)
                        for c in range(TC):
                            last = mm3(ps[:, b + c, 0:width], hTh[:, k, c * P:(c + 1) * P], hTl[:, k, c * P:(c + 1) * P],
                                       hi[:, kk, :], lo[:, kk, :], k == 0, k == DK - 1)
                    last.then_inc(chunk_used, 1)
            pe.wait_ge(sem("cq_made"), TC)
            for k in range(4):
                if k >= 2:
                    pe.wait_ge(sem("cq_scaled"), k - 1)
                for c in range(TC):
                    last = pe.transpose(ps[:, 6 + k % 2, c * P:(c + 1) * P], xn[:, c, k * P:(k + 1) * P], ident[:, :])
                last.then_inc(sem("cq_turned"), 1)
            pe.wait_ge(sem("ckv_made"), TC)
            pe.wait_ge(sem("cache_in"), 32)
            for k in range(2):
                for c in range(KC):
                    last = pe.transpose(ps[:, k, c * P:(c + 1) * P], ckv[:, c, k * P:(k + 1) * P], ident[:, :])
                last.then_inc(sem("ck_turned"), 1)
            pe.wait_ge(sem("lat_split"), 4)

            def keys(n, L):
                s = kv_chunk(n)
                wait_parts(pe, s, L(3))
                hi, lo = parts(s, 512, 2)
                for c in range(KC):
                    for k in range(2):
                        last = mm3(ps[:, 4 + c, :], ckTh[:, k, c * P:(c + 1) * P], ckTl[:, k, c * P:(c + 1) * P],
                                   hi[:, k, :], lo[:, k, :], k == 0, k == 1)
                last.then_inc(chunk_used, 1)

            def queries(n, L):
                s = kv_chunk(n) + 1
                wait_parts(pe, s, L(3))
                hi, lo = parts(s, 384, 4)
                for c in range(TC):
                    for k in range(4):
                        last = mm3(ps[:, c, 0:384], cqTh[:, k, c * P:(c + 1) * P], cqTl[:, k, c * P:(c + 1) * P],
                                   hi[:, k, :], lo[:, k, :], k == 0, k == 3)
                last.then_inc(chunk_used, 1)

            def scores(n, L, after):
                pe.wait_ge(sem("k_scaled"), at(n + 1, L(1)))
                for h in range(2):
                    for c in range(KC):
                        pe.transpose(ps[:, 6 + h, c * P:(c + 1) * P], k_sb[:, c, h, :], ident[:, :])
                if after:
                    pe.wait_ge(sem("att_y"), at(3 * (n - 1) + 2, L(3)))
                else:
                    pe.wait_ge(sem("q_copied"), 1)
                for c in range(KC):
                    last = pe.transpose(ps[:, 0, c * P:(c + 1) * P], krh[:, c, :, :].rearrange("p a b -> p (a b)"), ident[:, :])
                last.then_inc(sem("k_turned"), 1)
                pe.wait_ge(sem("q_scaled"), at(n + 1, L(1)))
                if after:
                    pe.wait_ge(sem("att_y"), at(3 * (n - 1) + 3, L(3)))
                for h in range(2):
                    for c in range(TC):
                        pe.transpose(ps[:, 1 + h, c * P:(c + 1) * P], q_sb[:, 2 * c + h, 0:P], ident[:, :])
                for c in range(TC):
                    last = pe.transpose(ps[:, 3, c * P:(c + 1) * P],
                                        qr[:, 0, 2 * c:2 * c + 2, :].rearrange("p a b -> p (a b)"), ident[:, :])
                last.then_inc(sem("q_turned"), 1)
                pe.wait_ge(sem("kT_made"), at(3 * n + 3, L(3)))
                pe.wait_ge(sem("rT_made"), at(2 * n + 2, L(2)))
                for h in range(2):
                    r0, r1 = RD * h, RD * (h + 1)
                    for c in range(TC):
                        a, b = ((0, P), (P, 4 * P), (0, 3 * P))[c]
                        k0, k1 = (0, P) if c == 0 else (P, KC * P)
                        o = ps[:, 2 * h + c // 2, a:b]
                        pe.matmul(o, QB[:, h, c * P:(c + 1) * P], KT[:, h, k0:k1], start=True, stop=False)
                        last = pe.matmul(o, QB[r0:r1, 2, c * P:(c + 1) * P], KR[r0:r1, k0:k1], start=False, stop=True)
                    last.then_inc(sem("scored"), 1)

            def attend(n, i, g=None, more=True):
                L = turns(g)
                if more:
                    pe.wait_ge(sem("att_y"), at(3 * n + 1, L(3)))
                    keys(n + 1, L)
                    pe.wait_ge(sem("exp_made"), at(6 * n + 6, L(6)))
                    queries(n + 1, L)
                    pe.wait_ge(sem("k_copied"), at(2 * n + 4, L(2)))
                for h in range(2):
                    pe.wait_ge(sem("p_made"), at(6 * n + 3 * h + 3, L(6)))
                    for c in (1, 2):
                        for k in range(3):
                            o = P * (2 * k + c - 1)
                            pe.transpose(ps[:, 4 + 2 * h + o // 512, o % 512:o % 512 + P],
                                         pr[:, h, P + 3 * P * (c - 1) + k * P:2 * P + 3 * P * (c - 1) + k * P], ident[:, :])
                    pe.transpose(ps[:, 5 + 2 * h, 2 * P:3 * P], pr[:, h, 0:P], ident[:, :]).then_inc(sem("p_turned"), 1)
                for h in range(2):
                    pe.wait_ge(sem("pT_hi"), at(2 * n + h + 1, L(2)))
                    pe.wait_ge(sem("pT_lo"), at(2 * n + h + 1, L(2)))
                    pe.matmul(ps[:, 3 + h, 0:P], v_sb[:, i, 0, h, :], pT[:, h, 6 * P:7 * P], start=True, stop=True)
                    for k in range(3):
                        last = pe.matmul(ps[:, 3 + h, P:T], v_sb[:, i, k + 1, h, :], pT[:, h, 2 * P * k:2 * P * (k + 1)],
                                         start=k == 0, stop=k == 2)
                    last.then_inc(sem("o_made"), 1)
                s = kv_chunk(n + 1) + 2 if more else MOE - 1
                wait_parts(pe, s, L(3))
                if more:
                    pe.wait_ge(sem("q_copied"), at(n + 2, L(1)))
                    pe.wait_ge(sem("q_square"), at(n + 2, L(1)))
                pe.wait_ge(sem("oT_lo"), at(2 * n + 2, L(2)))
                hi, lo = parts(s, D, 2)
                for c in range(TC):
                    for b in range(2):
                        for h in range(2):
                            last = mm3(ps[:, 2 * c + b, :], oTh[:, h, c * P:(c + 1) * P], oTl[:, h, c * P:(c + 1) * P],
                                       hi[:, h, b * 512:(b + 1) * 512], lo[:, h, b * 512:(b + 1) * 512], h == 0, h == 1)
                    last.then_inc(sem("out_made") if c < 2 else chunk_used, 1)
                if more:
                    scores(n + 1, L, True)

            keys(0, turns())
            queries(0, turns())
            scores(0, turns(), False)
            with pe.Fori(0, NPAIR // 2 - 1) as g:
                attend(0, 0, g)
                attend(1, 1, g)
            attend(NPAIR - 2, 0)
            attend(NPAIR - 1, 1, more=False)

            norm_pe(pe, "moe")
            pe.wait_ge(sem("att_y"), TC * NPAIR + 1)
            pe.wait_ge(sem("router_in"), 16)
            for k in range(DK):
                pe.wait_ge(sem("moe_modulated"), 2 * k + 2)
                last = pe.matmul(ps[0:NE, 5, 0:T], router[:, k, :], hf[:, k, :], start=k == 0, stop=k == DK - 1)
            last.then_inc(sem("logit_rows"), 1)
            for c in range(TC):
                if c == TC - 1:
                    pe.wait_ge(sem("logit_copied"), 1)
                    for b in range(TC):
                        last = pe.transpose(ps[:, 6, b * NE:(b + 1) * NE], lgT[:, b * P:(b + 1) * P], ident[0:NE, 0:NE])
                    last.then_inc(sem("logits_made"), 1)
                for k in range(DK):
                    last = pe.transpose(ps[:, 2 * c + k // 4, k % 4 * P:k % 4 * P + P], hf[:, k, c * P:(c + 1) * P], ident[:, :])
            last.then_inc(sem("tok_turned"), 1)
            pe.wait_ge(sem("gap_made"), 1)
            M = rt[:, 6, :, :]
            pe.matmul(ps[:, 7, 0:TC * NE], before[:, :], M.rearrange("p c e -> p (c e)"), start=True, stop=False)
            for b in range(TC - 1):
                last = pe.matmul(ps[:, 7, (b + 1) * NE:TC * NE], ones[:, :],
                                 M[:, b:b + 1, :].to_broadcast([P, TC - 1 - b, NE]) if b < TC - 2 else M[:, b, :],
                                 start=False, stop=b == TC - 2)
            last.then_inc(sem("ranked"), 1)
            for b in range(TC):
                last = pe.matmul(ps[:, 6, TC * NE:(TC + 1) * NE], ones[:, :], M[:, b, :], start=b == 0, stop=b == TC - 1)
            last.then_inc(sem("counted"), 1)
            pe.wait_ge(sem("tok_made"), TC)
            pe.wait_ge(sem("moe_const"), 10)

            def scatter():
                for c in range(TC):
                    for h in range(2):
                        o = ps[:, (0, 2, 6)[c] + h, :]
                        pe.matmul(o, selT[:, c * P:(c + 1) * P], yh[:, h * 512:(h + 1) * 512], start=True, stop=False)
                        last = pe.matmul(o, selT[:, c * P:(c + 1) * P], yl[:, h * 512:(h + 1) * 512], start=False, stop=True)
                    last.then_inc(sem("scattered"), 1)

            def tile(t):
                L = (t, TILE_CH)
                pe.wait_ge(sem("sel_made"), at(3, (t, 3)))
                for k in range(DK):
                    for c in range(TC):
                        last = pe.matmul(ps[:, 4 + k // 4, k % 4 * P:k % 4 * P + P], xn[:, c, k * P:(k + 1) * P], sel[:, c, :],
                                         start=c == 0, stop=c == TC - 1)
                last.then_inc(sem("gathered"), 1)
                pe.wait_ge(sem("y_lo"), at(1, (t, 1)))
                scatter()
                pe.wait_ge(sem("xg_lo"), at(1, (t, 1)))
                for c in range(TC):
                    last = pe.transpose(ps[:, 4, c * P:(c + 1) * P], sel[:, c, :], ident[:, :])
                last.then_inc(sem("sel_turned"), 1)

                def turn(g):
                    if g == 1:
                        pe.wait_ge(sem("selT_made"), at(1, (t, 1)))
                    pe.wait_ge(sem("hm_made"), at(g + 2, (t, 3)))
                    if g == 2:
                        pe.wait_ge(sem("hg_lo"), at(1, (t, 3)))
                    for i in range(4):
                        last = pe.transpose(ps[:, 5 - g % 2, i * P:(i + 1) * P], hm[:, g % 2, i * P:(i + 1) * P], ident[:, :])
                    last.then_inc(sem("hm_turned"), 1)

                for k in range(TILE_CH):
                    s = MOE + k
                    wait_parts(pe, s, L)
                    if k in (0, 4):
                        pe.wait_ge(sem("y_added"), at(k // 4 + 1, (t, 3)))
                    if k == 8:
                        pe.wait_ge(sem("hm_made"), at(2, (t, 3)))
                    if k == 12:
                        pe.wait_ge(sem("y_added"), at(3, (t, 3)))
                    if k >= 12 and k % 2 == 0:
                        pe.wait_ge(sem("hg_lo"), at((k - 12) // 2 + 1, (t, 3)))
                    if k < 12:
                        b = 2 * (k // 4 % 2) + k // 2 % 2
                        hi, lo = parts(s, 512, 4)
                        for i in range(4):
                            kk = 4 * (k % 2) + i
                            last = mm3(ps[:, b, :], xgh[:, kk, :], xgl[:, kk, :], hi[:, i, :], lo[:, i, :],
                                       kk == 0, kk == DK - 1)
                    else:
                        hi, lo = parts(s, D, 2)
                        for i in range(2):
                            f = 2 * (k - 12) + i
                            for h in range(2):
                                last = mm3(ps[:, 6 + h, :], hgh[:, f, :], hgl[:, f, :], hi[:, i, h * 512:(h + 1) * 512],
                                           lo[:, i, h * 512:(h + 1) * 512], f == 0, f == FE // P - 1)
                    last.then_inc(chunk_used, 1)
                    if k in (5, 9, 13):
                        turn(k // 4 - 1)

            with pe.Fori(0, NE) as e:
                tile(e)
            pe.wait_ge(sem("tab_ready"), 1)
            more = pe.value_load(tab[0:1, 0:1], min_val=0, max_val=NX)
            with pe.Fori(0, NX) as j:
                with pe.If(j < more):
                    tile(j + NE)
            pe.wait_ge(sem("y_lo"), at(1, (more + NE, 1)))
            scatter()


_OUTS = ["y_prompt", "y_sample", "new_ckv", "new_krope"]


def shape_tables(inputs):
    n = inputs["x_sample"].shape[1]
    rd = inputs["cache_krope"].shape[-1]
    ax = rd // 2
    pos = np.arange(n)
    inv = np.float32(ROPE_BASE) ** (-np.arange(0, ax, 2, dtype=np.float32) / np.float32(ax))
    ang = np.stack([(pos // GRID_W).astype(np.float32)[:, None] * inv, (pos % GRID_W).astype(np.float32)[:, None] * inv], 1)
    cos, sin = np.cos(ang), np.sin(ang)
    keys = inputs["x_prompt"].shape[1] + n + inputs["cache_ckv"].shape[2]
    tab = np.zeros((2, keys, rd), np.float32)
    tab[0] = 1.0
    p = inputs["x_prompt"].shape[1]
    tab[0, p:p + n] = np.stack([cos, cos], 2).reshape(n, rd)
    tab[1, p:p + n] = np.stack([-sin, sin], 2).reshape(n, rd)
    comb = np.array([[1, 0], [0, 1], [1, 1]], np.float32)
    return {"rope_tab": tab, "comb_tab": comb}


def kernel(**inputs):
    import concourse.bacc as bacc
    from concourse.bass_utils import run_bass_kernel_spmd

    nc = bacc.Bacc("TRN2", target_bir_lowering=False, num_devices=1)
    given = {**inputs, **shape_tables(inputs)}
    arrays = {f"in_{n}": np.ascontiguousarray(a) for n, a in given.items()}
    d = {n: nc.dram_tensor(f"in_{n}", arrays[f"in_{n}"].shape, F32, kind="ExternalInput").ap() for n in given}
    (b, seq, dm), (db, dseq, _) = inputs["x_prompt"].shape, inputs["x_sample"].shape
    _, nm, _, rank = inputs["cache_ckv"].shape
    shapes = [(b, seq, dm), (db, dseq, dm), (b, nm, seq, rank), (b, nm, seq, inputs["cache_krope"].shape[-1])]
    out = {n: nc.dram_tensor(f"out_{n}", s, F32, kind="ExternalOutput").ap() for n, s in zip(_OUTS, shapes)}
    hybrid_conv_mla_diffusion_step(nc, d, out)
    r = run_bass_kernel_spmd(nc, [arrays], core_ids=[0])
    return tuple(r.results[0][f"out_{n}"] for n in _OUTS)
```
